# Optimizing a Trainium2 kernel written in Bass

```python
import jax, jax.numpy as jnp
from jax import lax
import numpy as np

D_MODEL = 1024
BATCH = 1
SEQ = 1024
DEPTH = 1

D_MIX = D_MODEL
HEAD_DIM = 64
W_CONV = D_MIX // 4
W_SGU = D_MIX // 4
W_LRU = D_MIX // 2
H_CONV = W_CONV // HEAD_DIM
H_SGU = W_SGU // HEAD_DIM
H_LRU = W_LRU // HEAD_DIM
D_IN = 3 * W_CONV + 2 * W_SGU + 2 * W_LRU
CONV_A_WIDTH = 3
CONV_C_WIDTH = 4
CHUNK = 128
RGLRU_C = 8.0
N_EXPERTS = 32
TOP_K = 4
D_FF_EXPERT = D_MODEL
SWIGLU_LIMIT = 7.0
SWIGLU_ALPHA = 1.702
MOE_BLOCK = 128
N_MOD = 6
EPS = 1e-6

kernel_name = 'hybrid_conv_sgu_rglru_moe_adaln'

def rms_normalize(x):
    xf = x.astype(jnp.float32)
    return xf * lax.rsqrt(jnp.mean(xf * xf, axis=-1, keepdims=True) + EPS)

def rms_norm(x, g):
    return (rms_normalize(x) * g.astype(jnp.float32)).astype(x.dtype)

def layer_norm(x, g, b):
    xf = x.astype(jnp.float32)
    xc = xf - jnp.mean(xf, axis=-1, keepdims=True)
    y = xc * lax.rsqrt(jnp.mean(xc * xc, axis=-1, keepdims=True) + EPS)
    return (y * g.astype(jnp.float32) + b.astype(jnp.float32)).astype(x.dtype)

def causal_depthwise_conv(z, w):
    k_width = w.shape[0]
    seq = z.shape[1]
    zp = jnp.pad(z, ((0, 0), (k_width - 1, 0), (0, 0)))
    y = zp[:, 0:seq] * w[0]
    for k in range(1, k_width):
        y = y + zp[:, k:k + seq] * w[k]
    return y

def short_conv_mixer(b_gate, c_gate, v, conv_w):
    return b_gate * causal_depthwise_conv(c_gate * v, conv_w)

def chunked_spatial_gating(z, sgu_w, sgu_b, ln_g, ln_b):
    bsz, seq, _ = z.shape
    z = jax.nn.gelu(z)
    u, v = jnp.split(z, 2, axis=-1)
    v = layer_norm(v, ln_g, ln_b).reshape(bsz, seq // CHUNK, CHUNK, H_SGU, HEAD_DIM)
    causal = jnp.tril(jnp.ones((CHUNK, CHUNK), dtype=bool))
    w = jnp.where(causal[None], sgu_w, jnp.zeros((), sgu_w.dtype))
    mixed = jnp.einsum('hts,bnshd->bnthd', w, v) + jnp.transpose(sgu_b)[:, :, None]
    return u * mixed.reshape(bsz, seq, W_SGU)

def rg_lru(x, gate_w, gate_b, lam):
    bsz, seq, _ = x.shape
    xh = x.reshape(bsz, seq, H_LRU, HEAD_DIM)
    gates = jnp.einsum('bshi,ghij->gbshj', xh, gate_w) + gate_b[:, None, None]
    gates = jax.nn.sigmoid(gates.astype(jnp.float32)).reshape(2, bsz, seq, W_LRU)
    r, i = gates[0], gates[1]
    log_a = -RGLRU_C * r * jax.nn.softplus(-lam.astype(jnp.float32))
    a = jnp.exp(log_a)
    b = x.astype(jnp.float32) * i * jnp.sqrt(-jnp.expm1(2.0 * log_a))

    def combine(left, right):
        a_l, b_l = left
        a_r, b_r = right
        return a_l * a_r, a_r * b_l + b_r

    _, h = lax.associative_scan(combine, (a, b), axis=1)
    return h.astype(x.dtype)

def recurrent_branch(gate_in, x_in, conv_w, conv_b, gate_w, gate_b, lam):
    xr = causal_depthwise_conv(x_in, conv_w) + conv_b
    return jax.nn.gelu(gate_in) * rg_lru(xr, gate_w, gate_b, lam)

def hybrid_mixer(h, w_in, conv_a_w, sgu_w, sgu_b, sgu_ln_g, sgu_ln_b, conv_c_w, conv_c_b,
                 rglru_gate_w, rglru_gate_b, rglru_lambda, mix_norm_g, w_out):
    z = jnp.einsum('bsd,dp->bsp', h, w_in)
    cuts = [W_CONV, 2 * W_CONV, 3 * W_CONV, 3 * W_CONV + 2 * W_SGU, 3 * W_CONV + 2 * W_SGU + W_LRU]
    z_b, z_c, z_v, z_s, z_g, z_x = jnp.split(z, cuts, axis=-1)
    y_conv = short_conv_mixer(z_b, z_c, z_v, conv_a_w)
    y_sgu = chunked_spatial_gating(z_s, sgu_w, sgu_b, sgu_ln_g, sgu_ln_b)
    y_lru = recurrent_branch(z_g, z_x, conv_c_w, conv_c_b, rglru_gate_w, rglru_gate_b, rglru_lambda)
    y = jnp.concatenate([rms_normalize(y_conv), rms_normalize(y_sgu), rms_normalize(y_lru)], axis=-1)
    y = (y * mix_norm_g.astype(jnp.float32)).astype(h.dtype)
    return jnp.einsum('bsm,md->bsd', y, w_out)

def clamped_swiglu_expert(xb, w1, b1, w2, b2):
    hgu = xb @ w1 + b1
    g, u = jnp.split(hgu, 2, axis=-1)
    g = jnp.minimum(g, SWIGLU_LIMIT)
    u = jnp.clip(u, -SWIGLU_LIMIT, SWIGLU_LIMIT)
    return ((u + 1.0) * (g * jax.nn.sigmoid(SWIGLU_ALPHA * g))) @ w2 + b2

def moe_ffn(h, router_w, router_b, w1, b1, w2, b2):
    bsz, seq, d = h.shape
    n_tok = bsz * seq
    xt = h.reshape(n_tok, d)
    logits = xt.astype(jnp.float32) @ router_w.astype(jnp.float32) + router_b.astype(jnp.float32)
    top_logits, top_idx = lax.top_k(logits, TOP_K)
    top_w = jax.nn.softmax(top_logits, axis=-1)
    n_assign = n_tok * TOP_K
    flat_e = top_idx.reshape(n_assign)
    order = jnp.argsort(flat_e)
    sorted_e = flat_e[order]
    sorted_tok = (order // TOP_K).astype(jnp.int32)
    sorted_w = top_w.reshape(n_assign)[order]
    counts = jnp.bincount(flat_e, length=N_EXPERTS)
    padded = (counts + MOE_BLOCK - 1) // MOE_BLOCK * MOE_BLOCK
    pad_end = jnp.cumsum(padded)
    pad_start = pad_end - padded
    grp_start = jnp.cumsum(counts) - counts
    rank = jnp.arange(n_assign) - grp_start[sorted_e]
    slot = pad_start[sorted_e] + rank
    n_blocks = (n_assign + MOE_BLOCK - 1) // MOE_BLOCK + N_EXPERTS
    n_slots = n_blocks * MOE_BLOCK
    slot_tok = jnp.full((n_slots,), n_tok, jnp.int32).at[slot].set(sorted_tok)
    slot_w = jnp.zeros((n_slots,), jnp.float32).at[slot].set(sorted_w)
    x_pad = jnp.concatenate([xt, jnp.zeros((1, d), xt.dtype)], axis=0)
    x_blocks = x_pad[slot_tok].reshape(n_blocks, MOE_BLOCK, d)
    block_e = jnp.minimum(
        jnp.searchsorted(pad_end, jnp.arange(n_blocks) * MOE_BLOCK, side='right'), N_EXPERTS - 1)

    def run_block(args):
        xb, e = args
        return clamped_swiglu_expert(xb, w1[e], b1[e], w2[e], b2[e])

    y = lax.map(run_block, (x_blocks, block_e)).reshape(n_slots, d)
    y = y * slot_w[:, None].astype(y.dtype)
    out = jnp.zeros((n_tok + 1, d), y.dtype).at[slot_tok].add(y)[:n_tok]
    return out.reshape(bsz, seq, d)

def decoder_layer(x, c, norm1_g, norm2_g, w_ada, b_ada, w_in, conv_a_w, sgu_w, sgu_b, sgu_ln_g,
                  sgu_ln_b, conv_c_w, conv_c_b, rglru_gate_w, rglru_gate_b, rglru_lambda,
                  mix_norm_g, w_out, router_w, router_b, expert_w1, expert_b1, expert_w2, expert_b2):
    mod = (c @ w_ada + b_ada)[:, None, :]
    shift1, scale1, gate1, shift2, scale2, gate2 = jnp.split(mod, N_MOD, axis=-1)
    h = rms_norm(x, norm1_g) * (1.0 + scale1) + shift1
    x = x + gate1 * hybrid_mixer(h, w_in, conv_a_w, sgu_w, sgu_b, sgu_ln_g, sgu_ln_b, conv_c_w,
                                 conv_c_b, rglru_gate_w, rglru_gate_b, rglru_lambda, mix_norm_g, w_out)
    h = rms_norm(x, norm2_g) * (1.0 + scale2) + shift2
    x = x + gate2 * moe_ffn(h, router_w, router_b, expert_w1, expert_b1, expert_w2, expert_b2)
    return x

def setup_inputs(seed: int = 0) -> dict:
    key = jax.random.key(seed)
    ks = jax.random.split(key, 32)

    def nrm(k, shape, scale):
        return scale * jax.random.normal(k, shape, jnp.float32)

    u = jax.random.uniform(ks[16], (DEPTH, W_LRU), jnp.float32, minval=0.9, maxval=0.999)
    a0 = u ** (1.0 / RGLRU_C)
    rglru_lambda = jnp.log(a0) - jnp.log1p(-a0)
    return {
        'x': nrm(ks[0], (BATCH, SEQ, D_MODEL), 1.0),
        'c': nrm(ks[1], (BATCH, D_MODEL), 1.0),
        'norm1_g': 1.0 + nrm(ks[2], (DEPTH, D_MODEL), 0.02),
        'norm2_g': 1.0 + nrm(ks[3], (DEPTH, D_MODEL), 0.02),
        'w_ada': nrm(ks[4], (DEPTH, D_MODEL, N_MOD * D_MODEL), 0.2 * D_MODEL ** -0.5),
        'b_ada': nrm(ks[5], (DEPTH, N_MOD * D_MODEL), 0.02),
        'w_in': nrm(ks[6], (DEPTH, D_MODEL, D_IN), D_MODEL ** -0.5),
        'conv_a_w': nrm(ks[7], (DEPTH, CONV_A_WIDTH, W_CONV), CONV_A_WIDTH ** -0.5),
        'sgu_w': nrm(ks[8], (DEPTH, H_SGU, CHUNK, CHUNK), CHUNK ** -0.5),
        'sgu_b': 1.0 + nrm(ks[9], (DEPTH, H_SGU, CHUNK), 0.1),
        'sgu_ln_g': 1.0 + nrm(ks[10], (DEPTH, W_SGU), 0.02),
        'sgu_ln_b': nrm(ks[11], (DEPTH, W_SGU), 0.02),
        'conv_c_w': nrm(ks[12], (DEPTH, CONV_C_WIDTH, W_LRU), CONV_C_WIDTH ** -0.5),
        'conv_c_b': nrm(ks[13], (DEPTH, W_LRU), 0.02),
        'rglru_gate_w': nrm(ks[14], (DEPTH, 2, H_LRU, HEAD_DIM, HEAD_DIM), HEAD_DIM ** -0.5),
        'rglru_gate_b': nrm(ks[15], (DEPTH, 2, H_LRU, HEAD_DIM), 0.02),
        'rglru_lambda': rglru_lambda,
        'mix_norm_g': 1.0 + nrm(ks[17], (DEPTH, D_MIX), 0.02),
        'w_out': nrm(ks[18], (DEPTH, D_MIX, D_MODEL), D_MIX ** -0.5),
        'router_w': nrm(ks[19], (DEPTH, D_MODEL, N_EXPERTS), D_MODEL ** -0.5),
        'router_b': nrm(ks[20], (DEPTH, N_EXPERTS), 0.01),
        'expert_w1': nrm(ks[21], (DEPTH, N_EXPERTS, D_MODEL, 2 * D_FF_EXPERT), D_MODEL ** -0.5),
        'expert_b1': nrm(ks[22], (DEPTH, N_EXPERTS, 2 * D_FF_EXPERT), 0.01),
        'expert_w2': nrm(ks[23], (DEPTH, N_EXPERTS, D_FF_EXPERT, D_MODEL), D_FF_EXPERT ** -0.5),
        'expert_b2': nrm(ks[24], (DEPTH, N_EXPERTS, D_MODEL), 0.01),
        'final_norm_g': 1.0 + nrm(ks[25], (D_MODEL,), 0.02),
    }

def reference(x, c, norm1_g, norm2_g, w_ada, b_ada, w_in, conv_a_w, sgu_w, sgu_b, sgu_ln_g,
              sgu_ln_b, conv_c_w, conv_c_b, rglru_gate_w, rglru_gate_b, rglru_lambda, mix_norm_g,
              w_out, router_w, router_b, expert_w1, expert_b1, expert_w2, expert_b2, final_norm_g):
    for l in range(DEPTH):
        x = decoder_layer(x, c, norm1_g[l], norm2_g[l], w_ada[l], b_ada[l], w_in[l], conv_a_w[l],
                          sgu_w[l], sgu_b[l], sgu_ln_g[l], sgu_ln_b[l], conv_c_w[l], conv_c_b[l],
                          rglru_gate_w[l], rglru_gate_b[l], rglru_lambda[l], mix_norm_g[l], w_out[l],
                          router_w[l], router_b[l], expert_w1[l], expert_b1[l], expert_w2[l],
                          expert_b2[l])
    return rms_norm(x, final_norm_g)


_drawn_inputs = setup_inputs


def setup_inputs(seed=0):
    import zlib

    import numpy as np

    out = dict(_drawn_inputs(seed))
    spreads = {}
    factors = {'norm1_g': 7.444,
     'norm2_g': 5.266,
     'sgu_b': 5.975,
     'sgu_ln_g': 30.708,
     'sgu_ln_b': 33.997,
     'conv_c_b': 3.699,
     'rglru_gate_b': 8.0,
     'mix_norm_g': 8.0,
     'router_b': 7.367,
     'expert_b1': 25.751,
     'expert_b2': 64.0,
     'final_norm_g': 7.87}
    for name, (base, spread) in spreads.items():
        noise = np.random.default_rng([zlib.crc32(name.encode()), seed]).standard_normal(out[name].shape)
        drawn = base * np.exp(spread * noise) if base else spread * noise
        out[name] = __import__('jax').numpy.asarray(drawn.astype(out[name].dtype))
    for name, factor in factors.items():
        out[name] = (out[name] * factor).astype(out[name].dtype)
    return out
```

```python
import concourse.bass as bass
from concourse import mybir
from contextlib import ExitStack

P = 128
BANK = 512


def decoder_kernel(nc, x, c, norm1_g, norm2_g, w_ada, b_ada, w_in, conv_a_w, sgu_w, sgu_b, sgu_ln_g,
                   sgu_ln_b, conv_c_w, conv_c_b, gate_w, gate_b, lam, mix_g, w_out, router_w,
                   router_b, w1, b1, w2, b2, final_g, out):
    f32, f32r, bf16 = mybir.dt.float32, mybir.dt.float32r, mybir.dt.bfloat16
    i32, u32 = mybir.dt.int32, mybir.dt.uint32
    ALU, ACT, AX = mybir.AluOpType, mybir.ActivationFunctionType, mybir.AxisListType
    ds = bass.ds

    SEQ, D = x.shape[1], x.shape[2]
    TT, KT = SEQ // P, D // P
    E = router_w.shape[2]
    TOPK = 4
    FF = w2.shape[2]
    WC = conv_a_w.shape[2]
    WL = conv_c_w.shape[2]
    LJ, CJ = WL // P, WC // P
    NMOD = 6
    EPS = 1e-6
    LIMIT, ALPHA = 7.0, 1.702
    GELU_C, GELU_A = 0.7978845608028654, 0.044715
    PASS = 2 * P
    NPASS = E + SEQ * TOPK // PASS
    NBLK = 2 * (NPASS + 1)
    KU = KT // 2
    UNIT = KU * BANK
    PADROW = SEQ

    mod_d = nc.dram_tensor("mod_d", (NMOD * D,), f32, kind="Internal").ap()
    x1_d = nc.dram_tensor("x1_d", (SEQ, D), f32, kind="Internal").ap()
    h2_d = nc.dram_tensor("h2_d", (SEQ + P, D), f32, kind="Internal").ap()
    acc_d = nc.dram_tensor("acc_d", (SEQ + P, D), f32, kind="Internal").ap()
    spare_d = nc.dram_tensor("spare_d", (SEQ + P, 2), f32, kind="Internal").ap()
    zero_d = nc.dram_tensor("zero_d", (SEQ + P, 2), f32, kind="Internal").ap()
    slot_d = nc.dram_tensor("slot_d", (P * NBLK, 2), i32, kind="Internal").ap()
    pass_d = nc.dram_tensor("pass_d", (P, 2), i32, kind="Internal").ap()

    xf = x[0]
    outf = out[0]

    ctx = ExitStack()
    with ctx:
        def sb(name, shape, dt, where=ctx):
            return where.enter_context(nc.sbuf_tensor(name, shape, dt))

        def sem(name):
            return ctx.enter_context(nc.semaphore(name))

        rawA = sb("rawA", [P, 3, UNIT], f32)
        whi = sb("whi", [P, 3, KU, BANK], f32r)
        wlo = sb("wlo", [P, 3, KU, BANK], f32r)
        ident = sb("ident", [P, P], f32)
        idx_tab = sb("idx_tab", [P, NBLK], u32)
        wgt_tab = sb("wgt_tab", [P, NBLK], f32)
        pass_tab = sb("pass_tab", [1, 2 * P], i32)
        tiny = sb("tiny", [P, 3], f32)
        idx_g = sb("idx_g", [P, 2], u32)
        idx_s = sb("idx_s", [P, 2], u32)
        wcur = sb("wcur", [P, 2], f32)
        xpad = sb("xpad", [P, 2], f32)
        mhalf = sb("mhalf", [P, TT], f32)

        front = ExitStack()
        hTh = sb("hTh", [P, KT, SEQ], f32r, front)
        hTl = sb("hTl", [P, KT, SEQ], f32r, front)
        yT = sb("yT", [P, KT, SEQ], f32, front)
        T = sb("T", [P, 5, SEQ], f32, front)
        ones = sb("ones", [P, P], f32, front)
        ccol = sb("ccol", [P, KT], f32, front)
        gateW = sb("gateW", [P, 2, LJ, P], f32, front)
        gateB = sb("gateB", [P, 2, LJ], f32, front)
        gateBh = sb("gateBh", [P, 2, LJ], f32, front)
        lamc = sb("lamc", [P, LJ], f32, front)
        sp = sb("sp", [P, 6, LJ], f32, front)
        cw = sb("cw", [P, 4, LJ], f32, front)
        cb = sb("cb", [P, LJ], f32, front)
        caw = sb("caw", [P, 3, CJ], f32, front)
        mixg = sb("mixg", [P, KT], f32, front)
        sgW = sb("sgW", [P, 4, P], f32, front)
        sgB = sb("sgB", [P, 4], f32, front)
        acc = sb("acc", [P, BANK], f32, front)
        ss = sb("ss", [P, TT], f32, front)
        rs = sb("rs", [P, TT], f32, front)
        bnst = sb("bnst", [P, TT, 6], f32, front)
        mv = sb("mv", [P, TT, 2], f32, front)
        ssq = sb("ssq", [P, KT, TT], f32, front)
        rg = sb("rg", [P, 3, TT], f32, front)
        modrow = sb("modrow", [1, 2, BANK], f32, front)

        flat = yT[:, :, :].rearrange("p k s -> p (k s)")
        tail0 = 3 * SEQ

        def carve(n, dt=f32):
            nonlocal tail0
            a = flat[:, tail0:tail0 + n]
            tail0 += n
            return a if dt == f32 else a.bitcast(dt)

        rw = carve(KT * E).rearrange("p (k e) -> p k e", e=E)
        rb = carve(E)
        h2T = [carve(D).rearrange("p (k s) -> p k s", s=P) for _ in range(2)]
        lg = carve(TT * E).rearrange("p (t e) -> p t e", e=E)
        v8 = carve(TT * 8).rearrange("p (t k) -> p t k", k=8)
        i8 = carve(TT * 8, u32).rearrange("p (t k) -> p t k", k=8)
        i8f = carve(TT * TOPK).rearrange("p (t k) -> p t k", k=TOPK)
        dv = carve(TT * TOPK).rearrange("p (t k) -> p t k", k=TOPK)
        w4 = carve(TT * TOPK).rearrange("p (t k) -> p t k", k=TOPK)
        sm = carve(TT)
        rsm = carve(TT)
        iotaE = carve(E)
        iotaEi = carve(E, i32)
        mask = carve(TT * E).rearrange("p (t e) -> p t e", e=E)
        maskb = carve(TT * E // 2, bf16).rearrange("p (t e) -> p t e", e=E)
        Ub = carve(P // 2, bf16)
        onesb = carve(P // 2, bf16)
        cnt = carve(E)
        npe = carve(E)
        tmpe = carve(E)
        onee = carve(E)
        endp = carve(E)
        begp = carve(E)
        slot = carve(TT * E).rearrange("p (t e) -> p t e", e=E)
        slf = carve(TT * TOPK)
        sli = carve(TT * TOPK, i32)
        blki = carve(TT * TOPK, i32)
        remi = carve(TT * TOPK, i32)
        loci = carve(TT * TOPK, i32)
        pair = carve(TT * TOPK * 2, i32).rearrange("p (n c) -> p n c", c=2)
        tok = carve(TT, i32)
        pidi = carve(1, i32)
        pid = carve(1)
        pm = carve(4 * E).rearrange("p (a e) -> p a e", e=E)
        pcol = carve(4)
        pcoli = carve(2, i32)
        WdT = carve(P)
        assert tail0 <= KT * SEQ
        OH = T[:, 3, :].rearrange("p (n e) -> p n e", e=E)
        WOH = T[:, 4, :].rearrange("p (n e) -> p n e", e=E)
        Wd = T[:, 2, 0:TT * E].rearrange("p (t e) -> p t e", e=E)
        init_tab = T[:, 2, 512:512 + 2 * NBLK].bitcast(i32).rearrange("p (b c) -> p b c", c=2)
        b2s = T[0:E, 0, :]
        stage = T[:, 4, :].rearrange("p (a n) -> p a n", a=2)
        lng = T[:, 4, 0:2 * WC].rearrange("p (a n) -> p a n", a=2)

        front.close()

        held = ExitStack()
        rawB = sb("rawB", [P, 3, UNIT], f32, held)
        whi3 = sb("whi3", [P, KU, BANK], f32r, held)
        wlo3 = sb("wlo3", [P, KU, BANK], f32r, held)
        b1s = sb("b1s", [P, 2, BANK], f32, held)
        back = ExitStack()
        xg = sb("xg", [P, 2, D], f32, back)
        xTh = sb("xTh", [P, 2, KT, P], f32r, back)
        xTl = sb("xTl", [P, 2, KT, P], f32r, back)
        HTh = sb("HTh", [P, 2, KT, P], f32r, back)
        HTl = sb("HTl", [P, 2, KT, P], f32r, back)
        g_sb = sb("g_sb", [P, 2, BANK], f32, back)
        u_sb = sb("u_sb", [P, 2, BANK], f32, back)
        th = sb("th", [P, 2, BANK], f32, back)
        y_sb = sb("y_sb", [P, 2, D], f32, back)
        back.close()
        last = ExitStack()
        fx = sb("fx", [P, 3, D], f32, last)
        fa = sb("fa", [P, 3, D], f32, last)
        fsq = sb("fsq", [P, D], f32, last)
        fmod = sb("fmod", [P, 2, D], f32, last)
        fss = sb("fss", [P, TT], f32, last)
        frs = sb("frs", [P, TT], f32, last)
        last.close()
        held.close()

        bk = [ctx.enter_context(nc.psum_tensor(f"bank{i}", [P, BANK], f32)) for i in range(8)]

        s_const = sem("s_const")
        s_small = sem("s_small")
        s_raw = [sem(f"s_raw{i}") for i in range(3)]
        s_used = sem("s_used")
        s_adap = sem("s_adap")
        s_adam = sem("s_adam")
        s_adac = sem("s_adac")
        s_adab = sem("s_adab")
        s_adad = [sem("s_adad0"), sem("s_adad1")]
        s_brow = [sem("s_brow0"), sem("s_brow1")]
        s_bc = sem("s_bc")
        s_A = sem("s_A")
        s_x = [sem("s_x0"), sem("s_x1")]
        s_sq = sem("s_sq")
        s_rp = sem("s_rp")
        s_h0 = sem("s_h0")
        s_h = sem("s_h")
        s_tp = sem("s_tp")
        s_thi = sem("s_thi")
        s_tlo = sem("s_tlo")
        s_hi = sem("s_hi")
        s_z = sem("s_z")
        s_ze = sem("s_ze")
        s_par = sem("s_par")
        s_lng = sem("s_lng")
        s_sgt = sem("s_sgt")
        s_sgc = sem("s_sgc")
        s_sa = sem("s_sa")
        s_sd = sem("s_sd")
        s_sp = sem("s_sp")
        s_sm = sem("s_sm")
        s_st = sem("s_st")
        s_se = sem("s_se")
        s_la = sem("s_la")
        s_ld = sem("s_ld")
        s_lg = sem("s_lg")
        s_ls = sem("s_ls")
        s_ca = sem("s_ca")
        s_cd = sem("s_cd")
        s_rg = sem("s_rg")
        s_rgp = sem("s_rgp")
        s_yh = sem("s_yh")
        s_yl = sem("s_yl")
        s_o = sem("s_o")
        s_oa = sem("s_oa")
        s_od = sem("s_od")
        s_xo = [sem("s_xo0"), sem("s_xo1")]
        s_x1 = [sem("s_x10"), sem("s_x11")]
        s_bc2 = sem("s_bc2")
        s_A2 = sem("s_A2")
        s_x2 = [sem("s_x20"), sem("s_x21")]
        s_sq2 = sem("s_sq2")
        s_rp2 = sem("s_rp2")
        s_g0 = sem("s_g0")
        s_g = sem("s_g")
        s_h2d = [sem("s_h2d0"), sem("s_h2d1")]
        s_pad = sem("s_pad")
        s_tp2 = sem("s_tp2")
        s_tc2 = sem("s_tc2")
        s_lgm = sem("s_lgm")
        s_lgd = sem("s_lgd")
        s_r = sem("s_r")
        s_re = sem("s_re")
        s_rc = sem("s_rc")
        s_rk = sem("s_rk")
        s_wdt = sem("s_wdt")
        s_wdc = sem("s_wdc")
        s_b2 = sem("s_b2")
        s_b2m = sem("s_b2m")
        s_b2c = sem("s_b2c")
        s_b2d = [sem("s_b2d0"), sem("s_b2d1")]
        s_tab0 = sem("s_tab0")
        s_scat = sem("s_scat")
        s_tab = sem("s_tab")
        s_pt = sem("s_pt")
        s_ptl = sem("s_ptl")
        s_tabc = sem("s_tabc")
        e_raw = [sem(f"e_raw{i}") for i in range(6)]
        e_hi = sem("e_hi")
        e_lo = sem("e_lo")
        e_lop = sem("e_lop")
        e_unit = sem("e_unit")
        e_b1 = [sem("e_b10"), sem("e_b11")]
        e_main = sem("e_main")
        e_t = sem("e_t")
        e_g = sem("e_g")
        e_u = sem("e_u")
        e_th = sem("e_th")
        e_gs = sem("e_gs")
        e_H = sem("e_H")
        e_htp = sem("e_htp")
        e_hth = sem("e_hth")
        e_htl = sem("e_htl")
        e_xtp = sem("e_xtp")
        e_xth = sem("e_xth")
        e_xtl = sem("e_xtl")
        e_main2 = sem("e_main2")
        e_y = sem("e_y")
        e_idx = sem("e_idx")
        e_w = sem("e_w")
        e_gat = sem("e_gat")
        e_scat = sem("e_scat")
        e_free = sem("e_free")
        e_go = sem("e_go")
        f_bc = sem("f_bc")
        f_x = [sem(f"f_x{i}") for i in range(3)]
        f_d = sem("f_d")
        f_e = sem("f_e")
        f_a = sem("f_a")
        f_p = sem("f_p")
        f_o = [sem(f"f_o{i}") for i in range(3)]
        e_end = sem("e_end")

        SMALL = 16 * 19
        N_S, N_LD, N_LA, N_CD, N_CA = 5, 14, 11, 4, 3
        R_MASK, R_WD, R_RANK, R_SLOT, R_PASS = 7, 12, 24, 33, 44
        POOL_UNITS = (5, 10)
        TERMS = 9
        PAR_DONE = 2 + 5 + (TERMS - 1) + 5
        ZEROED = 3

        MIX = ["S"] + [("L", j) for j in range(LJ // 2)] + [("C", j) for j in range(CJ)]
        order = [("ada", n, h) for n in range(4) for h in range(2)]
        rest = [("ada", n, h) for n in range(4, NMOD * D // BANK) for h in range(2)]
        for i, m in enumerate(MIX):
            order += [("mix", i, h) for h in range(2)]
            order += rest[4 * i:4 * i + 4] if i + 1 < len(MIX) else rest[4 * i:]
        order += [("out", n, h) for n in range(2) for h in range(2)]
        split = [u for u in order if u[0] != "ada"]
        NF = len(order)
        ADA = [n for k, n, h in order if k == "ada" and h == 0]

        def columns(i):
            m = MIX[i]
            if m == "S":
                return [(3 * WC, 2 * WC)]
            base = 3 * WC + 2 * WC
            if m[0] == "L":
                return [(base + WL + 2 * P * m[1], 2 * P), (base + 2 * P * m[1], 2 * P)]
            return [(WC * a + P * m[1], P) for a in range(3)]

        def raw_count(u):
            return 16 * sum(dmas(order[v]) for v in range(u % 3, u + 1, 3))

        def dmas(unit):
            return len(columns(unit[1])) if unit[0] == "mix" else 1

        POINTS = {"start": ["a"] * 4 + [0, 1], "h": ["a"] * 2 + [2], "gating": [3],
                  "mixing": ["a"] * 2 + [4], "lru1": [5] + ["a"] * 2 + [6], "lru3": [7] + ["a"] * 2 + [8],
                  "conv0": [9, 10], "conv1": [11, 12], "out0": [13]}

        groups = []
        for i, m in enumerate(MIX):
            if m == "S":
                groups += [(i, "tok", t) for t in range(TT)]
            elif m[0] == "L":
                groups += [(i, a + jj, hf) for jj in range(2) for a in (0, 2) for hf in range(2)]
            else:
                groups += [(i, a, hf) for a in range(3) for hf in range(2)]
        first_group = [next(q for q, g in enumerate(groups) if g[0] == i) for i in range(len(MIX))]
        first_group.append(len(groups))
        HS = SEQ // 2

        def store_x1(eng, i):
            n, t = divmod(i, TT)
            eng.wait_ge(s_od, 4 * i + 4)
            eng.dma_start(x1_d[P * t:P * t + P, BANK * n:BANK * n + BANK], T[:, i % 2, BANK:2 * BANK])\
               .then_inc(s_x1[i % 2], 16)

        def store_h2(eng, t):
            eng.wait_ge(s_g, t + 1)
            eng.dma_start(h2_d[P * t:P * t + P, :], T[:, 2 + t % 2, :]).then_inc(s_h2d[t % 2], 16)

        def scatter(pool, blk):
            pool.indirect_dma_start(acc_d, bass.IndirectOffsetOnAxis(ap=idx_s[:, blk:blk + 1], axis=0),
                                    y_sb[:, blk, :], None, compute_op=ALU.add).then_inc(e_scat, 16)

        def raw5(p, v):
            return 32 * p + 16 * (v // 6 + 1)

        def lo_count(p, v):
            if v % 12 in POOL_UNITS:
                return e_lop, len(POOL_UNITS) * p + (len(POOL_UNITS) * (v // 12) + POOL_UNITS.index(v % 12) + 1)
            before = sum(w % 12 not in POOL_UNITS for w in range(v + 1))
            return e_lo, (12 - len(POOL_UNITS)) * p + before

        def unit_hi(v):
            return (whi[:, v % 4] if v % 4 < 3 else whi3[:, :, :]).rearrange("p k n -> p (k n)")

        def unit_lo(v):
            return (wlo[:, v % 4] if v % 4 < 3 else wlo3[:, :, :]).rearrange("p k n -> p (k n)")

        ctx.enter_context(nc.allow_non_contiguous_dma(reason="small parameters, channels on partitions"))
        block = ctx.enter_context(nc.Block())

        @block.sync
        def _(eng):
            small = 0

            def load(dst, src):
                nonlocal small
                eng.dma_start(dst, src).then_inc(s_small, 16)
                small += 16

            def unit(u):
                kind, n, h = order[u]
                if u >= 3:
                    eng.wait_ge(s_used, u - 2)
                dst = rawA[:, u % 3, :].rearrange("p (k n) -> p k n", n=BANK)
                if kind == "mix":
                    at = 0
                    for s0, wd in columns(n):
                        src = w_in[0].rearrange("(k p) n -> p k n", p=P)[:, KU * h:KU * h + KU, s0:s0 + wd]
                        eng.dma_start(dst[:, :, at:at + wd], src).then_inc(s_raw[u % 3], 16)
                        at += wd
                else:
                    w = (w_ada if kind == "ada" else w_out)[0].rearrange("(k p) n -> p k n", p=P)
                    eng.dma_start(dst, w[:, KU * h:KU * h + KU, BANK * n:BANK * n + BANK])\
                       .then_inc(s_raw[u % 3], 16)

            load(ccol[:, :], c[0].rearrange("(k p) -> p k", p=P))
            for u in range(3):
                unit(u)
            for d in range(2):
                for g in range(2):
                    load(gateW[64 * d:64 * d + 64, g, :, 64 * d:64 * d + 64],
                         gate_w[0, g].rearrange("(j a) i q -> i a j q", a=2)[:, d])
            for g in range(2):
                load(gateB[:, g, :], gate_b[0, g].rearrange("(j a) q -> (a q) j", a=2))
            load(lamc[:, :], lam[0].rearrange("(j p) -> p j", p=P))
            for k in range(4):
                load(cw[:, k, :], conv_c_w[0, k].rearrange("(j p) -> p j", p=P))
            load(cb[:, :], conv_c_b[0].rearrange("(j p) -> p j", p=P))
            for k in range(3):
                load(caw[:, k, :], conv_a_w[0, k].rearrange("(j p) -> p j", p=P))
            load(mixg[:, :], mix_g[0].rearrange("(j p) -> p j", p=P))
            load(sgB[:, :], sgu_b[0].rearrange("h t -> t h"))
            load(yT[:, 3, 0:4 * P].rearrange("p (h s) -> p h s", s=P), sgu_w[0].rearrange("h t s -> t h s"))
            assert small == SMALL
            for u in range(3, 8):
                unit(u)
            eng.wait_ge(s_adad[0], 32)
            eng.wait_ge(s_adad[1], 32)
            eng.dma_start(yT[:, 0, :], mod_d[0:D].rearrange("(a n) -> a n", a=1).to_broadcast([P, D]))\
               .then_inc(s_bc, 16)
            eng.dma_start(yT[:, 1, :], mod_d[D:2 * D].rearrange("(a n) -> a n", a=1).to_broadcast([P, D]))\
               .then_inc(s_bc, 16)
            eng.dma_start(yT[:, 2, :], norm1_g[0:1, :].to_broadcast([P, D])).then_inc(s_bc, 16)
            for u in range(8, NF):
                unit(u)
                if u == 10:
                    for t in range(TT):
                        if t >= 2:
                            eng.wait_ge(s_h0, t - 1)
                            eng.wait_ge(s_sq, t - 1)
                        eng.dma_start(T[:, t % 2, :], xf[P * t:P * t + P, :]).then_inc(s_x[t % 2], 16)
                    eng.wait_ge(s_sq, TT)
                    eng.dma_start(lng[:, 0, :], sgu_ln_g[0:1, :].to_broadcast([P, WC])).then_inc(s_lng, 16)
                    eng.dma_start(lng[:, 1, :], sgu_ln_b[0:1, :].to_broadcast([P, WC])).then_inc(s_lng, 16)
            eng.wait_ge(s_yl, KT)
            eng.wait_ge(s_ls, LJ + CJ)
            eng.wait_ge(s_adad[0], 16 * (NMOD * D // BANK // 2))
            eng.wait_ge(s_adad[1], 16 * (NMOD * D // BANK // 2))
            eng.dma_start(T[:, 4, :], mod_d[2 * D:3 * D].rearrange("(a n) -> a n", a=1).to_broadcast([P, D]))\
               .then_inc(s_bc2, 16)
            for n in range(2):
                for t in range(TT):
                    i = n * TT + t
                    if i >= 2:
                        eng.wait_ge(s_od, 4 * (i - 2) + 4)
                        eng.wait_ge(s_x1[i % 2], 16 * (i // 2))
                    eng.dma_start(T[:, 2 + i % 2, 0:BANK], xf[P * t:P * t + P, BANK * n:BANK * n + BANK])\
                       .then_inc(s_xo[i % 2], 16)
                    if i >= 1:
                        store_x1(eng, i - 1)
            store_x1(eng, 2 * TT - 1)
            for a, src in enumerate((mod_d[3 * D:4 * D].rearrange("(a n) -> a n", a=1),
                                     mod_d[4 * D:5 * D].rearrange("(a n) -> a n", a=1), norm2_g[0:1, :])):
                eng.dma_start(yT[:, a, :], src.to_broadcast([P, D])).then_inc(s_bc2, 16)
            eng.dma_start(rw, router_w[0].rearrange("(k p) e -> p k e", p=P)).then_inc(s_bc2, 16)
            eng.dma_start(rb, router_b[0:1, :].to_broadcast([P, E])).then_inc(s_bc2, 16)
            for i in range(2):
                eng.wait_ge(s_x1[i], 16 * TT)
            for t in range(TT):
                if t >= 2:
                    eng.wait_ge(s_g0, t - 1)
                    eng.wait_ge(s_sq2, t - 1)
                eng.dma_start(T[:, t % 2, :], x1_d[P * t:P * t + P, :]).then_inc(s_x2[t % 2], 16)
                if t >= 1:
                    store_h2(eng, t - 1)
            store_h2(eng, TT - 1)
            def w_unit(e, v):
                dst = (rawA if v % 6 < 3 else rawB)[:, v % 3, :].rearrange("p (k n) -> p k n", n=BANK)
                if v < 8:
                    ch, h = v // 2, v % 2
                    col = (ch % 2) * FF + (ch // 2) * BANK
                    w = w1[0, ds(e, 1)]
                else:
                    ch, h = (v - 8) % 2, (v - 8) // 2
                    col = ch * BANK
                    w = w2[0, ds(e, 1)]
                src = w.rearrange("a (k p) n -> p (a k) n", p=P)[:, KU * h:KU * h + KU, col:col + BANK]
                eng.dma_start(dst, src).then_inc(e_raw[v % 6], 16)

            def b1_chunk(e, ch):
                col = (ch % 2) * FF + (ch // 2) * BANK
                eng.dma_start(b1s[:, ch % 2, :], b1[0, ds(e, 1), col:col + BANK].to_broadcast([P, BANK]))\
                   .then_inc(e_b1[ch % 2], 16)

            eng.wait_ge(s_used, NF)
            eng.wait_ge(s_o, 6 * TT)
            for v in range(6):
                w_unit(0, v)
            for ch in range(2):
                b1_chunk(0, ch)
            eng.wait_ge(s_g0, TT)
            eng.wait_ge(s_h2d[0], 16 * (TT // 2))
            eng.wait_ge(s_h2d[1], 16 * (TT // 2))
            eng.wait_ge(s_rc, ZEROED)
            eng.dma_start(h2_d[SEQ:SEQ + P, :], T[:, 1, :]).then_inc(s_pad, 16)
            eng.dma_start(acc_d[SEQ:SEQ + P, :], T[:, 1, :]).then_inc(s_pad, 16)
            eng.dma_start(zero_d.rearrange("(p c) b -> p (c b)", p=P), T[:, 1, 0:2 * (SEQ + P) // P]).then_inc(s_pad, 16)
            eng.dma_start(slot_d.rearrange("(p b) c -> p b c", p=P), init_tab).then_inc(s_tab0, 16)
            eng.dma_start(b2s, b2[0]).then_inc(s_b2, 16)
            eng.wait_ge(s_r, R_PASS)
            eng.dma_start(pass_d, pcoli).then_inc(s_pt, 16)
            eng.wait_ge(s_pt, 16)
            eng.dma_start(pass_tab[0:1, :], pass_d.rearrange("p c -> (p c)").rearrange("(a n) -> a n", a=1))\
               .then_inc(s_ptl, 16)
            eng.wait_ge(s_scat, 16 * TT * TOPK)
            eng.dma_start(T[:, 3, 0:2 * NBLK].bitcast(i32).rearrange("p (b c) -> p b c", c=2),
                          slot_d.rearrange("(p b) c -> p b c", p=P)).then_inc(s_tab, 16)

            eng.wait_ge(s_ptl, 16)
            with eng.Fori(0, NPASS) as p:
                nb = eng.value_load(pass_tab[0:1, ds(2 * p + 1, 1)], min_val=0, max_val=2)
                with eng.If(nb > 0):
                    ex = eng.value_load(pass_tab[0:1, ds(2 * p, 1)], min_val=0, max_val=E - 1)
                    en = eng.value_load(pass_tab[0:1, ds(2 * p + 2, 1)], min_val=0, max_val=E - 1)
                    for w in range(6, 18):
                        eng.wait_ge(*lo_count(p, w - 6))
                        w_unit(ex if w < 12 else en, w % 12)
                        if w in (7, 9):
                            ch = (w - 3) // 2
                            eng.wait_ge(e_t, 8 * p + 2 * (ch - 2) + 2)
                            b1_chunk(ex, ch)
                        if w in (11, 13):
                            ch = (w - 11) // 2
                            eng.wait_ge(e_t, 8 * p + 2 * (ch + 2) + 2)
                            b1_chunk(en, ch)
            eng.wait_ge(e_end, 3)
            for i in range(2):
                src = (mod_d[5 * D:6 * D].rearrange("(a n) -> a n", a=1), final_g.rearrange("(a n) -> a n", a=1))[i]
                eng.dma_start(fmod[:, i, :], src.to_broadcast([P, D])).then_inc(f_bc, 16)
            for t in range(TT):
                if t >= 3:
                    eng.wait_ge(f_o[t % 3], 16 * (t // 3))
                eng.dma_start(fx[:, t % 3, :], x1_d[P * t:P * t + P, :]).then_inc(f_x[t % 3], 16)
                eng.dma_start(fa[:, t % 3, :], acc_d[P * t:P * t + P, :]).then_inc(f_x[t % 3], 16)
                if t >= 2:
                    eng.wait_ge(f_e, t - 1)
                    eng.dma_start(outf[P * (t - 2):P * (t - 1), :], fa[:, (t - 2) % 3, :]).then_inc(f_o[(t - 2) % 3], 16)
            for t in range(TT - 2, TT):
                eng.wait_ge(f_e, t + 1)
                eng.dma_start(outf[P * t:P * t + P, :], fa[:, t % 3, :]).then_inc(f_o[t % 3], 16)
            for i in range(3):
                eng.wait_ge(f_o[i], 16 * len(range(i, TT, 3)))

        @block.gpsimd
        def _(pool):
            pool.memset(ident[:, :], 0.0).then_inc(s_const, 1)
            pool.memset(ones[:, :], 1.0).then_inc(s_const, 1)
            pool.memset(mhalf[:, :], -0.5).then_inc(s_const, 1)
            pool.wait_ge(s_const, 3)
            pool.affine_select(out=ident[:, :], in_=ident[:, :], compare_op=ALU.not_equal, fill=1.0,
                               base=0, pattern=[[-1, P]], channel_multiplier=1).then_inc(s_const, 1)
            pool.wait_ge(s_small, SMALL)
            sg = yT[:, 3, 0:4 * P].rearrange("p (h s) -> p h s", s=P)
            pool.affine_select(out=sg, in_=sg, compare_op=ALU.is_ge, fill=0.0, base=0,
                               pattern=[[0, 4], [-1, P]], channel_multiplier=1).then_inc(s_const, 1)

            def power(dst, src, scale, done, step, n, e=1):
                pool.tensor_scalar(dst, src, scale, EPS, ALU.mult, ALU.add).then_inc(done, 1)
                pool.wait_ge(done, step + 1)
                pool.tensor_tensor(dst, dst, mhalf[:, 0:n], ALU.pow).then_inc(done, 1)

            for t in range(TT):
                pool.wait_ge(s_sq, t + 1)
                power(rs[:, t:t + 1], ss[:, t:t + 1], 1.0 / D, s_rp, 2 * t, 1)
            pool.wait_ge(s_sd, 4 * N_S + 2 * TT)
            pool.wait_ge(s_h0, TT)
            power(rs[:, :], mv[:, :, 1], 1.0, s_sp, 0, TT)
            pool.wait_ge(s_rg, 4)
            power(rg[:, 0, :], rg[:, 0, :], 1.0 / WC, s_rgp, 0, TT)
            power(rg[:, 1, :], ssq[:, 2, :], 1.0 / WC, s_rgp, 2, TT)
            power(rg[:, 2, :], rg[:, 2, :], 1.0 / WL, s_rgp, 4, TT)

            for t in range(TT):
                pool.wait_ge(s_sq2, t + 1)
                power(rs[:, t:t + 1], ss[:, t:t + 1], 1.0 / D, s_rp2, 2 * t, 1)
            pool.wait_ge(s_g0, TT)
            pool.wait_ge(s_h2d[0], 16 * (TT // 2))
            pool.wait_ge(s_tp2, 2 * TT)
            pool.memset(T[:, 1, :], 0.0).then_inc(s_rc, 1)
            pool.memset(init_tab[:, :, 1], 0).then_inc(s_rc, 1)
            pool.iota(init_tab[:, :, 0], pattern=[[0, NBLK]], base=PADROW, channel_multiplier=1).then_inc(s_rc, 1)
            pool.iota(iotaEi, pattern=[[1, E]], base=0, channel_multiplier=0).then_inc(s_rc, 1)
            pool.iota(tok, pattern=[[P, TT]], base=0, channel_multiplier=1).then_inc(s_rc, 1)
            pool.iota(pidi, pattern=[[0, 1]], base=0, channel_multiplier=1).then_inc(s_rc, 1)
            pool.memset(onesb, 1.0).then_inc(s_rc, 1)
            pool.memset(onee, 1.0).then_inc(s_rc, 1)
            pool.wait_ge(s_rc, 8)
            pool.affine_select(out=Ub, in_=onesb, compare_op=ALU.is_gt, fill=0.0, base=0,
                               pattern=[[1, P]], channel_multiplier=-1).then_inc(s_rc, 1)
            pool.wait_ge(s_r, R_SLOT)
            pool.wait_ge(s_tab0, 16)
            for n in range(TT * TOPK):
                pool.indirect_dma_start(slot_d, bass.IndirectOffsetOnAxis(ap=loci[:, n:n + 1].bitcast(u32), axis=0),
                                        pair[:, n, :], None).then_inc(s_scat, 16)

            def gather(blk):
                pool.indirect_dma_start(xg[:, blk, :], None, h2_d,
                                        bass.IndirectOffsetOnAxis(ap=idx_g[:, blk:blk + 1], axis=0))\
                    .then_inc(e_gat, 16)

            def lo(p, v):
                pool.wait_ge(e_hi, 12 * p + v + 1)
                pool.tensor_tensor(unit_lo(v), (rawA if v % 6 < 3 else rawB)[:, v % 3, :], unit_hi(v).bitcast(f32),
                                   ALU.subtract).then_inc(e_lop, 1)

            pool.wait_ge(s_tabc, 2)
            pool.wait_ge(s_pad, 48)
            pool.tensor_copy(idx_g[:, :], idx_tab[:, 0:2]).then_inc(e_idx, 1)
            pool.wait_ge(e_idx, 1)
            gather(0)
            gather(1)
            for i in range(2):
                if i:
                    pool.wait_ge(e_scat, 16)
                pool.indirect_dma_start(spare_d, bass.IndirectOffsetOnAxis(ap=idx_tab[:, NBLK - 1:NBLK], axis=0),
                                        wgt_tab[:, NBLK - 2:NBLK], None).then_inc(e_scat, 16)
            pool.wait_ge(e_scat, 32)
            pool.wait_ge(s_b2d[0], 16 * TT)
            pool.wait_ge(s_b2d[1], 16 * TT)
            pool.wait_ge(s_ptl, 16)
            with pool.Fori(0, NPASS) as p:
                nb = pool.value_load(pass_tab[0:1, ds(2 * p + 1, 1)], min_val=0, max_val=2)
                nbn = pool.value_load(pass_tab[0:1, ds(2 * p + 3, 1)], min_val=0, max_val=2)
                with pool.If(nb > 0):
                    pool.wait_ge(e_xtp, 4 * p + 4)
                    pool.wait_ge(e_gat, 32 * p + 32)
                    pool.tensor_copy(idx_g[:, :], idx_tab[:, ds(2 * p + 2, 2)]).then_inc(e_idx, 1)
                    pool.wait_ge(e_idx, p + 2)
                    pool.sem_inc(e_go, 1)
                    gather(0)
                    with pool.If(nbn == 2):
                        gather(1)
                    with pool.If(nbn < 2):
                        pool.indirect_dma_start(xpad[:, :], None, zero_d,
                                                bass.IndirectOffsetOnAxis(ap=idx_g[:, 1:2], axis=0))\
                            .then_inc(e_gat, 16)
                    lo(p, POOL_UNITS[0])
                    pool.wait_ge(e_scat, 32 * p + 32)
                    pool.sem_inc(e_free, 1)
                    pool.tensor_copy(idx_s[:, :], idx_tab[:, ds(2 * p, 2)]).then_inc(e_w, 1)
                    pool.tensor_copy(wcur[:, :], wgt_tab[:, ds(2 * p, 2)]).then_inc(e_w, 1)
                    lo(p, POOL_UNITS[1])
                with pool.If(nb == 2):
                    pool.wait_ge(e_w, 2 * p + 2)
                    pool.wait_ge(e_y, 4 * p + 4 + 3)
                    pool.sem_inc(e_go, 1)
                    scatter(pool, 0)
                    pool.wait_ge(e_y, 4 * p + 4 + 4)
                    pool.sem_inc(e_go, 1)
                    scatter(pool, 1)
                with pool.If(nb == 1):
                    pool.wait_ge(e_w, 2 * p + 2)
                    pool.wait_ge(e_y, 4 * p + 4 + 4)
                    pool.sem_inc(e_go, 1)
                    scatter(pool, 0)
                    pool.indirect_dma_start(spare_d, bass.IndirectOffsetOnAxis(ap=idx_s[:, 1:2], axis=0),
                                            wcur[:, :], None).then_inc(e_scat, 16)
                with pool.If(nb > 0):
                    with pool.If(nbn == 0):
                        pool.wait_ge(e_scat, 32 * p + 64)
                        pool.sem_inc(e_go, 1)
            pool.memset(tiny[:, 0:1], 0.0).then_inc(e_end, 1)

            pool.wait_ge(e_end, 3)
            for t in range(TT):
                pool.wait_ge(f_a, t + 1)
                power(frs[:, t:t + 1], fss[:, t:t + 1], 1.0 / D, f_p, 2 * t, 1)

        @block.scalar
        def _(act):
            A = nc.scalar.activation
            tok_at = lambda t: slice(P * t, P * t + P)
            half = lambda h: slice(HS * h, HS * h + HS)

            def hi_unit(i):
                u = order.index(split[i])
                act.wait_ge(s_raw[u % 3], raw_count(u))
                if i >= 3:
                    done = (i - 3) // 2
                    if done < len(MIX):
                        act.wait_ge(s_z, first_group[done + 1])
                    else:
                        act.wait_ge(s_o, 3 * TT)
                A(whi[:, i % 3].rearrange("p k n -> p (k n)"), rawA[:, u % 3, :], ACT.Copy).then_inc(s_hi, 1)

            def copy_group(q, dst):
                act.wait_ge(s_z, q + 1)
                A(dst, bk[q % 3][:, :], ACT.Copy).then_inc(s_ze, 1)

            act.wait_ge(s_par, 2)
            A(sp[:, 1, :], sp[:, 0, :], ACT.Exp, scale=-1.0).then_inc(s_sgc, 1)
            act.wait_ge(s_sgt, 1)
            A(sgW[:, :, :].rearrange("p h t -> p (h t)"), bk[7][:, :], ACT.Copy).then_inc(s_sgc, 1)

            rows = 0

            def stream(point):
                nonlocal rows
                for what in POINTS[point]:
                    if what != "a":
                        hi_unit(what)
                        continue
                    i, rows = rows, rows + 1
                    col = slice(BANK * ADA[i], BANK * ADA[i] + BANK)
                    if i >= 1:
                        act.wait_ge(s_adad[(i - 1) % 2], 16 * ((i - 1) // 2 + 1))
                    act.dma_start(modrow[0:1, 1, :], b_ada[0:1, col]).then_inc(s_brow[i % 2], 16)
                    act.wait_ge(s_adam, i + 1)
                    A(modrow[0:1, 0, :], bk[3][0:1, :], ACT.Copy).then_inc(s_adac, 1)
                    act.wait_ge(s_adab, i + 1)
                    act.dma_start(mod_d[col].rearrange("(a n) -> a n", a=1), modrow[0:1, 0, :])\
                       .then_inc(s_adad[i % 2], 16)

            stream("start")

            for t in range(TT + 1):
                if t < TT:
                    act.wait_ge(s_x[t % 2], 16 * (t // 2 + 1))
                    if t:
                        act.wait_ge(s_sq, t)
                    A(T[:, 4, :], T[:, t % 2, :], ACT.Square, accum_out=ss[:, t:t + 1]).then_inc(s_sq, 1)
                if t >= 1:
                    for h in range(2):
                        q = 2 * (t - 1) + h
                        act.wait_ge(s_tp, q + 1)
                        A(hTh[:, 4 * h:4 * h + 4, tok_at(t - 1)],
                          bk[4 + q % 4][:, :].rearrange("p (k s) -> p k s", s=P), ACT.Copy).then_inc(s_thi, 1)
            stream("h")

            for b in range(TT // 2):
                z, w = 2 * (b % 2), 2 * (b % 2) + 1
                if b == 0:
                    act.wait_ge(s_h0, TT)
                    act.wait_ge(s_tp, 2 * TT)
                if b >= 2:
                    act.wait_ge(s_sd, N_S * (b - 1))
                for t in (2 * b, 2 * b + 1):
                    copy_group(t, T[:, z, BANK * (t % 2):BANK * (t % 2) + BANK])
                act.wait_ge(s_ze, 2 * b + 2)
                A(T[:, w, :], T[:, z, :], ACT.Square).then_inc(s_sa, 1)
                act.wait_ge(s_sd, N_S * b + 2)
                A(T[:, w, :], T[:, w, :], ACT.Tanh, scale=GELU_C).then_inc(s_sa, 1)
                if b == 2:
                    stream("gating")
            stream("mixing")
            Y = T[:, 0:2, :].rearrange("p a (t n) -> p (a t) n", n=WC)
            act.wait_ge(s_sd, 4 * N_S + 3 * TT + 2 + 4)
            for t in range(TT):
                if t:
                    act.wait_ge(s_sa, 8 + t)
                A(T[:, 2, 0:WC], Y[:, t, :], ACT.Square, accum_out=ssq[:, 2, t:t + 1]).then_inc(s_sa, 1)
            for j in range(2):
                for h in range(2):
                    act.wait_ge(s_st, 2 * j + h + 1)
                    A(yT[:, CJ + j, half(h)], bk[4 + 2 * j + h][:, :], ACT.Copy).then_inc(s_se, 1)

            for j in range(LJ):
                q0 = first_group[1 + j // 2] + 4 * (j % 2)
                if j == 0:
                    act.wait_ge(s_sa, 8 + TT)
                    act.wait_ge(s_st, 4)
                else:
                    act.wait_ge(s_ld, N_LD * j)
                for h in range(2):
                    copy_group(q0 + h, T[:, 0, half(h)])
                for h in range(2):
                    copy_group(q0 + 2 + h, T[:, 4, half(h)])
                act.wait_ge(s_ze, q0 + 2)
                act.wait_ge(s_small, SMALL)
                if j:
                    act.wait_ge(s_lg, 2 * j)
                A(T[:, 1, :], T[:, 0, :], ACT.Identity, scale=cw[:, 3, j:j + 1], bias=cb[:, j:j + 1]).then_inc(s_la, 1)
                if j % 2:
                    stream(f"lru{j}")
                act.wait_ge(s_ld, N_LD * j + 3)
                act.wait_ge(s_par, PAR_DONE)
                act.wait_ge(s_lg, 2 * j + 1)
                for h in range(2):
                    A(T[:, 0, half(h)], bk[4 + h][:, :], ACT.Tanh, scale=0.5, bias=gateBh[:, 0, j:j + 1]).then_inc(s_la, 1)
                act.wait_ge(s_la, N_LA * j + 3)
                A(T[:, 0, :], T[:, 0, :], ACT.Tanh, scale=sp[:, 5, j:j + 1], bias=sp[:, 5, j:j + 1]).then_inc(s_la, 1)
                act.wait_ge(s_lg, 2 * j + 2)
                if j:
                    act.wait_ge(s_la, N_LA * j)
                for h in range(2):
                    A(T[:, 2, half(h)], bk[6 + h][:, :], ACT.Tanh, scale=0.5, bias=gateBh[:, 1, j:j + 1]).then_inc(s_la, 1)
                act.wait_ge(s_la, N_LA * j + 4)
                if j:
                    act.wait_ge(s_ls, j)
                A(T[:, 3, :], T[:, 0, :], ACT.Sqrt).then_inc(s_la, 1)
                act.wait_ge(s_ld, N_LD * j + 8)
                act.wait_ge(s_ze, q0 + 4)
                A(T[:, 3, :], T[:, 4, :], ACT.Square).then_inc(s_la, 1)
                act.wait_ge(s_ld, N_LD * j + 12)
                A(T[:, 3, :], T[:, 3, :], ACT.Tanh, scale=GELU_C).then_inc(s_la, 1)
                act.wait_ge(s_ld, N_LD * j + 14)
                A(T[:, 3, :], yT[:, 2 * CJ + j, :], ACT.Square).then_inc(s_la, 1)
                act.wait_ge(s_ls, j + 1)
                A(ssq[:, 2 * CJ + j, :], bk[4][:, 0:TT], ACT.Copy).then_inc(s_la, 1)

            for j in range(CJ):
                q0 = first_group[1 + LJ // 2 + j]
                if j == 0:
                    act.wait_ge(s_ld, N_LD * LJ)
                else:
                    act.wait_ge(s_cd, N_CD * j)
                for a in range(3):
                    for h in range(2):
                        copy_group(q0 + 2 * a + h, T[:, a, half(h)])
                act.wait_ge(s_cd, N_CD * j + 1)
                act.wait_ge(s_ls, LJ + j)
                A(T[:, 3, :], T[:, 1, :], ACT.Copy, scale=caw[:, 2, j:j + 1]).then_inc(s_ca, 1)
                stream(f"conv{j}")
                act.wait_ge(s_cd, N_CD * j + 4)
                if j:
                    act.wait_ge(s_ls, LJ + j)
                A(T[:, 4, :], yT[:, j, :], ACT.Square).then_inc(s_ca, 1)
                act.wait_ge(s_ls, LJ + j + 1)
                A(ssq[:, j, :], bk[4][:, 0:TT], ACT.Copy).then_inc(s_ca, 1)
            assert rows == len(ADA)

            act.wait_ge(s_z, len(groups))
            act.wait_ge(s_se, 4)
            for k in range(KT):
                A(hTh[:, k, :], yT[:, k, :], ACT.Copy, scale=mixg[:, k:k + 1]).then_inc(s_yh, 1)
            for i in range(2 * TT):
                n, t = divmod(i, TT)
                act.wait_ge(s_o, 3 * i + 1)
                act.wait_ge(s_rgp, 6)
                if i == 0:
                    act.wait_ge(s_yl, KT)
                    act.wait_ge(s_ca, N_CA * CJ)
                    act.wait_ge(s_ls, LJ + CJ)
                if i >= 2:
                    act.wait_ge(s_od, 4 * (i - 2) + 4)
                A(T[:, i % 2, 0:BANK], bk[3 * (i % 2)][:, :], ACT.Copy, scale=rg[:, 0, t:t + 1]).then_inc(s_oa, 1)
                if i == TT - 1:
                    stream("out0")

            act.wait_ge(s_od, 8 * TT)
            for t in range(TT + 1):
                if t < TT:
                    act.wait_ge(s_x2[t % 2], 16 * (t // 2 + 1))
                    if t:
                        act.wait_ge(s_sq2, t)
                    A(T[:, 4, :], T[:, t % 2, :], ACT.Square, accum_out=ss[:, t:t + 1]).then_inc(s_sq2, 1)
                if t >= 1:
                    for h in range(2):
                        q = 2 * (t - 1) + h
                        act.wait_ge(s_tp2, q + 1)
                        if h == 0 and t >= 3:
                            act.wait_ge(s_lgm, t - 2)
                        A(h2T[(t - 1) % 2][:, 4 * h:4 * h + 4, :], bk[q % 4][:, :].rearrange("p (k s) -> p k s", s=P),
                          ACT.Copy).then_inc(s_tc2, 1)
            def hi(p, v):
                act.wait_ge(e_raw[v % 6], raw5(p, v))
                w = v - 4
                if w == 8 or w == 9:
                    act.wait_ge(e_unit, 6 * p + w - 3)
                elif w == 10:
                    act.wait_ge(e_main2, 4 * p + 2)
                elif w >= 0 and w % 2 == 0:
                    act.wait_ge(e_unit, 6 * p + w // 2 + 1)
                elif w >= 0:
                    act.wait_ge(e_main, 8 * p + w + 1)
                src = (rawA if v % 6 < 3 else rawB)[:, v % 3, :]
                A(unit_hi(v), src, ACT.Copy).then_inc(e_hi, 1)

            def x_hi(p, blk):
                for h in range(2):
                    j = 2 * blk + h
                    act.wait_ge(e_xtp, 4 * p + j + 1)
                    A(xTh[:, blk, 4 * h:4 * h + 4, :], bk[4 + h][:, :].rearrange("p (k s) -> p k s", s=P),
                      ACT.Copy).then_inc(e_xth, 1)

            act.wait_ge(s_r, 1)
            A(w4.rearrange("p t k -> p (t k)"), dv.rearrange("p t k -> p (t k)"), ACT.Exp).then_inc(s_re, 1)
            for t in range(TT):
                if t in (1, 3, 5):
                    if t == 1:
                        act.wait_ge(s_o, 6 * TT)
                    hi(0, t // 2)
                act.wait_ge(s_wdt, t + 1)
                if t:
                    act.wait_ge(s_b2m, 2 * t)
                A(WdT[0:E, :], bk[7][0:E, 0:P], ACT.Copy).then_inc(s_wdc, 1)
                for n in range(2):
                    i = 2 * t + n
                    act.wait_ge(s_b2m, i + 1)
                    if i >= 2:
                        act.wait_ge(s_b2d[i % 2], 16 * (i // 2))
                    A(stage[:, i % 2, :], bk[5 + n][:, :], ACT.Copy).then_inc(s_b2c, 1)
                    act.wait_ge(s_b2c, i + 1)
                    act.dma_start(acc_d[P * t:P * t + P, BANK * n:BANK * n + BANK], stage[:, i % 2, :])\
                       .then_inc(s_b2d[i % 2], 16)

            act.sem_inc(e_y, 4)
            x_hi(0, 0)
            x_hi(0, 1)

            def body(p, nb, nbn):
                inc = 3 - nb
                at = lambda i, blk: 2 * i + (blk + 1) * inc
                blocks = range(nb)
                for v in range(12):
                    if v in (2, 6):
                        hi(p, v + 3)
                        i = (v - 2) // 4
                        for blk in blocks:
                            act.wait_ge(e_g, 4 * p + at(i, blk))
                            A(th[:, blk, :], g_sb[:, blk, :], ACT.Tanh, scale=ALPHA / 2).then_inc(e_th, inc)
                        continue
                    if v in (7, 9):
                        i = 0 if v == 7 else 1
                        for blk in blocks:
                            act.wait_ge(e_htp, 4 * p + at(i, blk))
                            A(HTh[:, blk, 4 * i:4 * i + 4, :], bk[6 + blk][:, :].rearrange("p (k s) -> p k s", s=P),
                              ACT.Copy).then_inc(e_hth, inc)
                    if v == 8:
                        x_hi(p + 1, 0)
                    if v == 11:
                        y_out(p, 0, nb)
                        with act.If(nbn == 2):
                            x_hi(p + 1, 1)
                        with act.If(nbn < 2):
                            act.wait_ge(e_xth, 4 * p + 6)
                            act.sem_inc(e_xth, 2)
                    hi(p, v + 3)
                y_out(p, 1, nb)

            def y_out(p, ch, nb):
                inc = 3 - nb
                for blk in range(nb):
                    act.wait_ge(e_main2, 4 * p + 2 * ch + (blk + 1) * inc)
                    act.wait_ge(e_w, 2 * p + 2)
                    act.wait_ge(e_free, p + 1)
                    A(y_sb[:, blk, BANK * ch:BANK * ch + BANK], bk[2 * ch + blk][:, :], ACT.Copy,
                      scale=wcur[:, blk:blk + 1]).then_inc(e_y, inc)

            with act.Fori(0, NPASS) as p:
                nb = act.value_load(pass_tab[0:1, ds(2 * p + 1, 1)], min_val=0, max_val=2)
                nbn = act.value_load(pass_tab[0:1, ds(2 * p + 3, 1)], min_val=0, max_val=2)
                with act.If(nb == 2):
                    body(p, 2, nbn)
                with act.If(nb == 1):
                    body(p, 1, nbn)
            A(tiny[:, 1:2], mhalf[:, 0:1], ACT.Copy).then_inc(e_end, 1)

            act.wait_ge(e_end, 3)
            for t in range(TT):
                act.wait_ge(f_d, 2 * t + 2)
                if t:
                    act.wait_ge(f_a, t)
                A(fsq[:, :], fx[:, t % 3, :], ACT.Square, accum_out=fss[:, t:t + 1]).then_inc(f_a, 1)

        @block.vector
        def _(dve):
            V = nc.vector
            half = lambda h: slice(HS * h, HS * h + HS)
            tok_at = lambda t: slice(P * t, P * t + P)
            used = 0
            lows = 0
            adap = 0

            def lo_unit():
                nonlocal used, lows
                assert order[used][0] != "ada", order[used]
                dve.wait_ge(s_hi, lows + 1)
                V.tensor_tensor(wlo[:, lows % 3].rearrange("p k n -> p (k n)"), rawA[:, used % 3, :],
                                whi[:, lows % 3].rearrange("p k n -> p (k n)").bitcast(f32),
                                ALU.subtract).then_inc(s_used, 1)
                used += 1
                lows += 1

            def ada_sum(i):
                nonlocal used, adap
                if i == 0:
                    dve.wait_ge(s_small, SMALL)
                else:
                    dve.wait_ge(s_adam, i)
                for h in range(2):
                    assert order[used] == ("ada", ADA[i], h), (order[used], i, h)
                    dve.wait_ge(s_raw[used % 3], raw_count(used))
                    for k in range(KU):
                        w = rawA[:, used % 3, BANK * k:BANK * k + BANK]
                        ck = ccol[:, KU * h + k:KU * h + k + 1]
                        if h == 0 and k == 0:
                            ins = V.tensor_scalar(acc[:, :], w, ck, None, ALU.mult)
                        else:
                            if k:
                                dve.wait_ge(s_adap, adap)
                            else:
                                dve.wait_ge(s_used, used)
                            ins = V.scalar_tensor_tensor(acc[:, :], w, ck, acc[:, :], ALU.mult, ALU.add)
                        if k < KU - 1:
                            ins.then_inc(s_adap, 1)
                            adap += 1
                    ins.then_inc(s_used, 1)
                    used += 1

            def ada_bias(i):
                dve.wait_ge(s_adac, i + 1)
                dve.wait_ge(s_brow[i % 2], 16 * (i // 2 + 1))
                V.tensor_tensor(modrow[0:1, 0, :], modrow[0:1, 0, :], modrow[0:1, 1, :], ALU.add).then_inc(s_adab, 1)

            sums = 0

            def stream(point):
                nonlocal sums
                due = None
                for what in POINTS[point] + [None]:
                    if what == "a":
                        ada_sum(sums)
                    if due is not None:
                        ada_bias(due)
                        due = None
                    if what == "a":
                        due, sums = sums, sums + 1
                    elif what is not None:
                        assert what == lows
                        lo_unit()

            V.memset(gateW[0:64, :, :, 64:P], 0.0)
            V.memset(gateW[64:P, :, :, 0:64], 0.0).then_inc(s_par, 1)
            dve.wait_ge(s_small, SMALL)
            V.scalar_tensor_tensor(sp[:, 0, :], lamc[:, :], -1.0, lamc[:, :], ALU.mult, ALU.max).then_inc(s_par, 1)
            stream("start")
            par = 2

            def plink(ins):
                nonlocal par
                ins.then_inc(s_par, 1)
                par += 1
                dve.wait_ge(s_par, par)

            dve.wait_ge(s_sgc, 1)
            plink(V.tensor_scalar(sp[:, 2, :], sp[:, 1, :], 2.0, None, ALU.add))
            plink(V.reciprocal(sp[:, 3, :], sp[:, 2, :]))
            plink(V.tensor_tensor(sp[:, 2, :], sp[:, 1, :], sp[:, 3, :], ALU.mult))
            plink(V.tensor_tensor(sp[:, 3, :], sp[:, 2, :], sp[:, 2, :], ALU.mult))
            plink(V.tensor_scalar(sp[:, 4, :], sp[:, 3, :], 1.0 / (2 * TERMS + 1), None, ALU.mult))
            for n in range(TERMS - 1, 0, -1):
                plink(V.scalar_tensor_tensor(sp[:, 4, :], sp[:, 4, :], 1.0 / (2 * n + 1), sp[:, 3, :], ALU.add, ALU.mult))
            plink(V.scalar_tensor_tensor(sp[:, 4, :], sp[:, 4, :], 1.0, sp[:, 2, :], ALU.add, ALU.mult))
            plink(V.tensor_scalar(sp[:, 5, :], lamc[:, :], -1.0, 0.0, ALU.mult, ALU.max))
            plink(V.scalar_tensor_tensor(sp[:, 5, :], sp[:, 4, :], 2.0, sp[:, 5, :], ALU.mult, ALU.add))
            plink(V.tensor_scalar(sp[:, 5, :], sp[:, 5, :], 2.0, None, ALU.mult))
            plink(V.tensor_scalar(gateBh[:, :, :], gateB[:, :, :], 0.5, None, ALU.mult))
            assert par == PAR_DONE, par

            dve.wait_ge(s_bc, 48)
            V.scalar_tensor_tensor(yT[:, 1, :], yT[:, 1, :], 1.0, yT[:, 2, :], ALU.add, ALU.mult).then_inc(s_A, 1)
            dve.wait_ge(s_A, 1)

            def h_low(t):
                for h in range(2):
                    q = 2 * t + h
                    dve.wait_ge(s_thi, q + 1)
                    V.tensor_tensor(hTl[:, 4 * h:4 * h + 4, tok_at(t)], bk[4 + q % 4][:, :].rearrange("p (k s) -> p k s", s=P),
                                    hTh[:, 4 * h:4 * h + 4, tok_at(t)].bitcast(f32), ALU.subtract).then_inc(s_tlo, 1)

            for t in range(TT):
                dve.wait_ge(s_rp, 2 * t + 2)
                dve.wait_ge(s_x[t % 2], 16 * (t // 2 + 1))
                if t >= 2:
                    dve.wait_ge(s_tp, 2 * (t - 2) + 2)
                V.scalar_tensor_tensor(T[:, 2 + t % 2, :], T[:, t % 2, :], rs[:, t:t + 1], yT[:, 1, :],
                                       ALU.mult, ALU.mult).then_inc(s_h0, 1)
                dve.wait_ge(s_h0, t + 1)
                V.tensor_tensor(T[:, 2 + t % 2, :], T[:, 2 + t % 2, :], yT[:, 0, :], ALU.add).then_inc(s_h, 1)
                if t >= 1:
                    h_low(t - 1)
            h_low(TT - 1)
            stream("h")

            U_ = yT[:, 2 * CJ:2 * CJ + 2, :].rearrange("p a (t n) -> p (a t) n", n=WC)
            V_ = yT[:, 2 * CJ + 2:2 * CJ + 4, :].rearrange("p a (t n) -> p (a t) n", n=WC)
            sd = 0

            def slink(ins):
                nonlocal sd
                ins.then_inc(s_sd, 1)
                sd += 1
                dve.wait_ge(s_sd, sd)

            for b in range(TT // 2):
                z, w = 2 * (b % 2), 2 * (b % 2) + 1
                dve.wait_ge(s_sa, 2 * b + 1)
                slink(V.tensor_scalar(T[:, w, :], T[:, w, :], GELU_A, 1.0, ALU.mult, ALU.add))
                slink(V.tensor_tensor(T[:, w, :], T[:, w, :], T[:, z, :], ALU.mult))
                dve.wait_ge(s_sa, 2 * b + 2)
                slink(V.scalar_tensor_tensor(T[:, w, :], T[:, w, :], 1.0, T[:, z, :], ALU.add, ALU.mult))
                g = T[:, w, :].rearrange("p (t n) -> p t n", n=2 * WC)
                slink(V.tensor_scalar(U_[:, 2 * b:2 * b + 2, :], g[:, :, 0:WC], 0.5, None, ALU.mult))
                slink(V.tensor_scalar(V_[:, 2 * b:2 * b + 2, :], g[:, :, WC:2 * WC], 0.5, None, ALU.mult))
                if b == 2:
                    stream("gating")
            stream("mixing")
            for t in range(TT):
                V.bn_stats(bnst[:, t, :], V_[:, t, :]).then_inc(s_sd, 1)
            sd += TT
            for t in range(TT):
                dve.wait_ge(s_sd, sd)
                V.bn_aggr(mv[:, t, :], bnst[:, t, :]).then_inc(s_sd, 1)
            sd += TT
            dve.wait_ge(s_sp, 2)
            for t in range(TT):
                V.tensor_scalar(V_[:, t, :], V_[:, t, :], mv[:, t, 0:1], rs[:, t:t + 1], ALU.subtract,
                                ALU.mult).then_inc(s_sd, 1)
            sd += TT
            dve.wait_ge(s_sd, sd)
            dve.wait_ge(s_lng, 32)
            slink(V.tensor_tensor(V_, V_, lng[:, 0:1, :].to_broadcast([P, TT, WC]), ALU.mult))
            slink(V.tensor_tensor(V_, V_, lng[:, 1:2, :].to_broadcast([P, TT, WC]), ALU.add))
            assert sd == 4 * N_S + 3 * TT + 2
            Y = T[:, 0:2, :].rearrange("p a (t n) -> p (a t) n", n=WC)
            for h in range(4):
                dve.wait_ge(s_sm, h + 1)
                V.scalar_tensor_tensor(Y[:, :, 64 * h:64 * h + 64], bk[4 + h][:, :].rearrange("p (t n) -> p t n", n=64),
                                       sgB[:, h:h + 1], U_[:, :, 64 * h:64 * h + 64], ALU.add,
                                       ALU.mult).then_inc(s_sd, 1)
            sd += 4

            N = SEQ
            for j in range(LJ):
                ld = N_LD * j

                def link(ins):
                    nonlocal ld
                    ins.then_inc(s_ld, 1)
                    ld += 1
                    dve.wait_ge(s_ld, ld)

                la = N_LA * j
                dve.wait_ge(s_la, la + 1)
                for k in (1, 2, 3):
                    link(V.scalar_tensor_tensor(T[:, 1, k:N], T[:, 0, 0:N - k], cw[:, 3 - k, j:j + 1], T[:, 1, k:N],
                                                ALU.mult, ALU.add))
                if j % 2:
                    stream(f"lru{j}")
                dve.wait_ge(s_la, la + 6)
                link(V.scalar_tensor_tensor(T[:, 2, :], T[:, 2, :], 1.0, T[:, 1, :], ALU.add, ALU.mult))
                dve.wait_ge(s_lg, 2 * j + 2)
                link(V.tensor_scalar(T[:, 1, :], T[:, 0, :], 1.0, None, ALU.add))
                link(V.reciprocal(T[:, 1, :], T[:, 1, :]))
                link(V.tensor_tensor(T[:, 2, :], T[:, 2, :], T[:, 1, :], ALU.mult))
                dve.wait_ge(s_la, la + 7)
                link(V.tensor_tensor(T[:, 2, :], T[:, 2, :], T[:, 3, :], ALU.mult))
                link(V.tensor_scalar(T[:, 0, :], T[:, 1, :], 2.0, -1.0, ALU.mult, ALU.add))
                link(V.tensor_tensor_scan(T[:, 1, :], T[:, 0, :], T[:, 2, :], 0.0, ALU.mult, ALU.add))
                dve.wait_ge(s_la, la + 8)
                link(V.tensor_scalar(T[:, 3, :], T[:, 3, :], GELU_A, 1.0, ALU.mult, ALU.add))
                link(V.tensor_tensor(T[:, 3, :], T[:, 3, :], T[:, 4, :], ALU.mult))
                dve.wait_ge(s_la, la + 9)
                link(V.scalar_tensor_tensor(T[:, 3, :], T[:, 3, :], 1.0, T[:, 4, :], ALU.add, ALU.mult))
                if j == 0:
                    dve.wait_ge(s_sm, 4)
                    dve.wait_ge(s_se, 4)
                link(V.scalar_tensor_tensor(yT[:, 2 * CJ + j, :], T[:, 3, :], 0.5, T[:, 1, :], ALU.mult, ALU.mult))
                assert ld == N_LD * (j + 1)

            for j in range(CJ):
                cd = N_CD * j
                q0 = first_group[1 + LJ // 2 + j]

                def clink(ins):
                    nonlocal cd
                    ins.then_inc(s_cd, 1)
                    cd += 1
                    dve.wait_ge(s_cd, cd)

                dve.wait_ge(s_ze, q0 + 6)
                clink(V.tensor_tensor(T[:, 1, :], T[:, 1, :], T[:, 2, :], ALU.mult))
                dve.wait_ge(s_ca, N_CA * j + 1)
                for k in (1, 2):
                    clink(V.scalar_tensor_tensor(T[:, 3, k:N], T[:, 1, 0:N - k], caw[:, 2 - k, j:j + 1], T[:, 3, k:N],
                                                 ALU.mult, ALU.add))
                stream(f"conv{j}")
                clink(V.tensor_tensor(yT[:, j, :], T[:, 3, :], T[:, 0, :], ALU.mult))

            dve.wait_ge(s_la, N_LA * LJ)
            dve.wait_ge(s_ca, N_CA * CJ)
            dve.wait_ge(s_sa, 8 + TT)
            V.tensor_tensor(rg[:, 0, :], ssq[:, 0, :], ssq[:, 1, :], ALU.add).then_inc(s_rg, 1)
            V.tensor_tensor(rg[:, 2, :], ssq[:, 4, :], ssq[:, 5, :], ALU.add).then_inc(s_rg, 1)
            for k in (6, 7):
                dve.wait_ge(s_rg, k - 4)
                V.tensor_tensor(rg[:, 2, :], rg[:, 2, :], ssq[:, k, :], ALU.add).then_inc(s_rg, 1)

            for k in range(KT):
                dve.wait_ge(s_yh, k + 1)
                V.scalar_tensor_tensor(hTl[:, k, :], yT[:, k, :], mixg[:, k:k + 1], hTh[:, k, :].bitcast(f32),
                                       ALU.mult, ALU.subtract).then_inc(s_yl, 1)
            for i in range(2 * TT):
                n, t = divmod(i, TT)
                od = 4 * i

                def olink(ins):
                    nonlocal od
                    ins.then_inc(s_od, 1)
                    od += 1
                    dve.wait_ge(s_od, od)

                tt = T[:, i % 2, 0:BANK]
                dve.wait_ge(s_oa, i + 1)
                dve.wait_ge(s_o, 3 * i + 3)
                olink(V.scalar_tensor_tensor(tt, bk[3 * (i % 2) + 1][:, :], rg[:, 1, t:t + 1], tt, ALU.mult, ALU.add))
                olink(V.scalar_tensor_tensor(tt, bk[3 * (i % 2) + 2][:, :], rg[:, 2, t:t + 1], tt, ALU.mult, ALU.add))
                dve.wait_ge(s_bc2, 16)
                olink(V.tensor_tensor(tt, tt, T[:, 4, BANK * n:BANK * n + BANK], ALU.mult))
                dve.wait_ge(s_xo[i % 2], 16 * (i // 2 + 1))
                if i >= 2:
                    dve.wait_ge(s_x1[i % 2], 16 * (i // 2))
                olink(V.tensor_tensor(T[:, i % 2, BANK:2 * BANK], tt, T[:, 2 + i % 2, 0:BANK], ALU.add))
                if i == TT - 1:
                    stream("out0")
            assert used == NF

            dve.wait_ge(s_bc2, 16 * 6)
            V.scalar_tensor_tensor(yT[:, 1, :], yT[:, 1, :], 1.0, yT[:, 2, :], ALU.add, ALU.mult).then_inc(s_A2, 1)
            dve.wait_ge(s_A2, 1)

            def logits(t):
                dve.wait_ge(s_lgm, t + 1)
                V.tensor_tensor(lg[:, t, :], bk[4 + t % 2][:, 0:E], rb, ALU.add).then_inc(s_lgd, 1)

            for t in range(TT):
                dve.wait_ge(s_rp2, 2 * t + 2)
                dve.wait_ge(s_x2[t % 2], 16 * (t // 2 + 1))
                if t >= 2:
                    dve.wait_ge(s_tp2, 2 * (t - 2) + 2)
                    dve.wait_ge(s_h2d[t % 2], 16 * (t // 2))
                V.scalar_tensor_tensor(T[:, 2 + t % 2, :], T[:, t % 2, :], rs[:, t:t + 1], yT[:, 1, :],
                                       ALU.mult, ALU.mult).then_inc(s_g0, 1)
                dve.wait_ge(s_g0, t + 1)
                V.tensor_tensor(T[:, 2 + t % 2, :], T[:, 2 + t % 2, :], yT[:, 0, :], ALU.add).then_inc(s_g, 1)
                if t >= 2:
                    logits(t - 2)
            logits(TT - 2)
            logits(TT - 1)

            dve.wait_ge(s_lgd, TT)
            for t in range(TT):
                V.max(v8[:, t, :], lg[:, t, :]).then_inc(s_lgd, 1)
            dve.wait_ge(s_lgd, 2 * TT)
            for t in range(TT):
                V.max_index(i8[:, t, :], v8[:, t, :], lg[:, t, :]).then_inc(s_lgd, 1)
            r = 0

            def link(ins):
                nonlocal r
                ins.then_inc(s_r, 1)
                r += 1
                dve.wait_ge(s_r, r)

            n3 = lambda ap: ap.rearrange("p t k -> p (t k)")
            NC = TT * TOPK
            link(V.tensor_tensor(dv, v8[:, :, 0:TOPK], v8[:, :, 0:1].to_broadcast([P, TT, TOPK]), ALU.subtract))
            dve.wait_ge(s_lgd, 3 * TT)
            link(V.tensor_copy(i8f, i8[:, :, 0:TOPK]))
            dve.wait_ge(s_rc, 9)
            link(V.tensor_copy(iotaE, iotaEi))
            link(V.tensor_copy(pid, pidi))
            dve.wait_ge(s_tp2, 2 * TT)
            dve.wait_ge(s_h2d[0], 16 * (TT // 2))
            dve.wait_ge(s_h2d[1], 16 * (TT // 2))
            link(V.tensor_tensor(OH, iotaE.rearrange("p (a e) -> p a e", a=1).to_broadcast([P, NC, E]),
                                 n3(i8f).rearrange("p (n a) -> p n a", a=1).to_broadcast([P, NC, E]), ALU.is_equal))
            link(V.tensor_reduce(mask, OH.rearrange("p (t k) e -> p t e k", k=TOPK), AX.X, ALU.add))
            link(V.tensor_copy(maskb, mask))
            assert r == R_MASK
            dve.wait_ge(s_re, 1)
            link(V.tensor_reduce(sm, w4, AX.X, ALU.add))
            link(V.reciprocal(rsm, sm))
            link(V.tensor_tensor(w4, w4, rsm.rearrange("p (t a) -> p t a", a=1).to_broadcast([P, TT, TOPK]), ALU.mult))
            link(V.tensor_tensor(WOH, OH, n3(w4).rearrange("p (n a) -> p n a", a=1).to_broadcast([P, NC, E]), ALU.mult))
            link(V.tensor_reduce(Wd, WOH.rearrange("p (t k) e -> p t e k", k=TOPK), AX.X, ALU.add))
            assert r == R_WD
            link(V.tensor_scalar(pair[:, :, 1].bitcast(f32), n3(w4), 0.5, None, ALU.mult))
            link(V.tensor_copy(pair[:, :, 0].rearrange("p (t k) -> p t k", k=TOPK),
                               tok.rearrange("p (t a) -> p t a", a=1).to_broadcast([P, TT, TOPK])))
            dve.wait_ge(s_rk, 2)
            link(V.tensor_copy(cnt, bk[7][:, 256:256 + E]))
            link(V.tensor_scalar(npe, cnt, float(PASS), 1.0, ALU.is_gt, ALU.add))
            for k in range(2, SEQ // PASS):
                link(V.tensor_scalar(tmpe, cnt, float(PASS * k), None, ALU.is_gt))
                link(V.tensor_tensor(npe, npe, tmpe, ALU.add))
            link(V.tensor_tensor_scan(endp, onee, npe, 0.0, ALU.mult, ALU.add))
            link(V.tensor_tensor(begp, endp, npe, ALU.subtract))
            link(V.tensor_scalar(tmpe, begp, float(PASS), None, ALU.mult))
            link(V.tensor_tensor(slot, bk[7][:, 0:TT * E].rearrange("p (t e) -> p t e", e=E),
                                 tmpe.rearrange("p (a e) -> p a e", a=1).to_broadcast([P, TT, E]), ALU.add))
            for k in range(TOPK):
                o = OH.rearrange("p (t k) e -> p t k e", k=TOPK)[:, :, k, :]
                link(V.tensor_tensor(o, o, slot, ALU.mult))
            link(V.tensor_reduce(slf, OH, AX.X, ALU.add))
            link(V.tensor_copy(sli, slf))
            link(V.tensor_single_scalar(blki, sli, 7, ALU.logical_shift_right))
            link(V.tensor_single_scalar(remi, sli, P - 1, ALU.bitwise_and))
            link(V.scalar_tensor_tensor(loci, remi, float(NBLK), blki, ALU.mult, ALU.add))
            assert r == R_SLOT, r
            link(V.tensor_scalar(pm[:, 0, :], endp, pid, None, ALU.is_le))
            link(V.tensor_scalar(pm[:, 1, :], begp, pid, None, ALU.is_le))
            link(V.tensor_tensor(pm[:, 1, :], pm[:, 1, :], pm[:, 0, :], ALU.subtract))
            link(V.tensor_tensor(pm[:, 2, :], tmpe, cnt, ALU.add))
            link(V.tensor_scalar(pcol[:, 2:3], pid, float(PASS), float(P), ALU.mult, ALU.add))
            link(V.tensor_scalar(pm[:, 2, :], pm[:, 2, :], pcol[:, 2:3], None, ALU.is_gt))
            link(V.scalar_tensor_tensor(pm[:, 2, :], pm[:, 2, :], 1.0, pm[:, 1, :], ALU.add, ALU.mult))
            link(V.tensor_reduce(pcol[:, 0:1], pm[:, 0, :], AX.X, ALU.add))
            link(V.tensor_reduce(pcol[:, 1:2], pm[:, 2, :], AX.X, ALU.add))
            link(V.tensor_scalar(pcol[:, 0:1], pcol[:, 0:1], float(E - 1), None, ALU.min))
            link(V.tensor_copy(pcoli, pcol[:, 0:2]))
            assert r == R_PASS, r
            def lo(p, v):
                if v % 12 in POOL_UNITS:
                    return
                dve.wait_ge(e_hi, 12 * p + v + 1)
                V.tensor_tensor(unit_lo(v), (rawA if v % 6 < 3 else rawB)[:, v % 3, :], unit_hi(v).bitcast(f32),
                                ALU.subtract).then_inc(e_lo, 1)

            for v in range(3):
                lo(0, v)
            dve.wait_ge(s_tab, 16)
            st = T[:, 3, 0:2 * NBLK].rearrange("p (b c) -> p b c", c=2)
            V.tensor_copy(idx_tab[:, :], st[:, :, 0].bitcast(u32)).then_inc(s_tabc, 1)
            V.tensor_copy(wgt_tab[:, :], st[:, :, 1]).then_inc(s_tabc, 1)

            def x_lo(p, blk):
                for h in range(2):
                    dve.wait_ge(e_xth, 4 * p + 2 * blk + h + 1)
                    V.tensor_tensor(xTl[:, blk, 4 * h:4 * h + 4, :], bk[4 + h][:, :].rearrange("p (k s) -> p k s", s=P),
                                    xTh[:, blk, 4 * h:4 * h + 4, :].bitcast(f32), ALU.subtract).then_inc(e_xtl, 1)

            x_lo(0, 0)
            x_lo(0, 1)

            def body(p, nb, nbn):
                inc = 3 - nb
                at = lambda i, blk: 2 * i + (blk + 1) * inc
                blocks = range(nb)

                def bias(ch, blk):
                    dve.wait_ge(e_main, 8 * p + at(ch, blk))
                    dve.wait_ge(e_b1[ch % 2], 32 * p + 16 * (ch // 2 + 1))
                    i = ch // 2
                    if ch % 2 == 0:
                        dst = g_sb
                    else:
                        dst = u_sb
                    V.tensor_tensor(dst[:, blk, :], bk[2 * (ch % 2) + blk][:, :], b1s[:, ch % 2, :],
                                    ALU.add).then_inc(e_t, inc)

                for v in range(12):
                    i = v // 4
                    if v in (2, 6):
                        for blk in blocks:
                            if i:
                                dve.wait_ge(e_H, 4 * p + at(0, blk))
                            bias(2 * i, blk)
                            dve.wait_ge(e_t, 8 * p + at(2 * i, blk))
                            V.tensor_scalar(g_sb[:, blk, :], g_sb[:, blk, :], LIMIT, None, ALU.min).then_inc(e_g, inc)
                    if v in (3, 7):
                        for blk in blocks:
                            dve.wait_ge(e_th, 4 * p + at(i, blk))
                            V.scalar_tensor_tensor(g_sb[:, blk, :], th[:, blk, :], 1.0, g_sb[:, blk, :],
                                                   ALU.add, ALU.mult).then_inc(e_gs, inc)
                    if v in (4, 8):
                        i -= 1
                        for blk in blocks:
                            bias(2 * i + 1, blk)
                            dve.wait_ge(e_t, 8 * p + at(2 * i + 1, blk))
                            V.tensor_scalar(u_sb[:, blk, :], u_sb[:, blk, :], LIMIT, -LIMIT, ALU.min,
                                            ALU.max).then_inc(e_u, inc)
                            dve.wait_ge(e_u, 4 * p + at(i, blk))
                            dve.wait_ge(e_gs, 4 * p + at(i, blk))
                            V.scalar_tensor_tensor(u_sb[:, blk, :], u_sb[:, blk, :], 1.0, g_sb[:, blk, :],
                                                   ALU.add, ALU.mult).then_inc(e_H, inc)
                    if v in (7, 9):
                        i = 0 if v == 7 else 1
                        for blk in blocks:
                            dve.wait_ge(e_hth, 4 * p + at(i, blk))
                            V.tensor_tensor(HTl[:, blk, 4 * i:4 * i + 4, :],
                                            bk[6 + blk][:, :].rearrange("p (k s) -> p k s", s=P),
                                            HTh[:, blk, 4 * i:4 * i + 4, :].bitcast(f32), ALU.subtract)\
                                .then_inc(e_htl, inc)
                    if v == 10:
                        x_lo(p + 1, 0)
                    if v == 11:
                        with dve.If(nbn == 2):
                            x_lo(p + 1, 1)
                        with dve.If(nbn < 2):
                            dve.wait_ge(e_xtl, 4 * p + 6)
                            dve.sem_inc(e_xtl, 2)
                    lo(p, v + 3)

            with dve.Fori(0, NPASS) as p:
                nb = dve.value_load(pass_tab[0:1, ds(2 * p + 1, 1)], min_val=0, max_val=2)
                nbn = dve.value_load(pass_tab[0:1, ds(2 * p + 3, 1)], min_val=0, max_val=2)
                with dve.If(nb == 2):
                    body(p, 2, nbn)
                with dve.If(nb == 1):
                    body(p, 1, nbn)
            V.tensor_copy(tiny[:, 2:3], mhalf[:, 0:1]).then_inc(e_end, 1)

            dve.wait_ge(f_bc, 32)
            def total(t):
                i = t % 3
                dve.wait_ge(f_x[i], 32 * (t // 3 + 1))
                V.tensor_tensor(fa[:, i, :], fa[:, i, :], fmod[:, 0, :], ALU.mult).then_inc(f_d, 1)
                dve.wait_ge(f_d, 2 * t + 1)
                V.tensor_tensor(fx[:, i, :], fx[:, i, :], fa[:, i, :], ALU.add).then_inc(f_d, 1)

            total(0)
            for t in range(TT):
                if t + 1 < TT:
                    total(t + 1)
                dve.wait_ge(f_p, 2 * t + 2)
                V.scalar_tensor_tensor(fa[:, t % 3, :], fx[:, t % 3, :], frs[:, t:t + 1], fmod[:, 1, :], ALU.mult,
                                       ALU.mult).then_inc(f_e, 1)

        @block.tensor
        def _(pe):
            mm = nc.tensor.matmul
            tok_at = lambda t: slice(P * t, P * t + P)
            half = lambda h: slice(HS * h, HS * h + HS)
            sums = 0
            ada_unit = [u for u, o in enumerate(order) if o[0] == "ada" and o[2] == 1]
            split_unit = [u for u, o in enumerate(order) if o[0] != "ada"]

            def stream(point):
                nonlocal sums
                for what in POINTS[point]:
                    if what == "a":
                        pe.wait_ge(s_used, ada_unit[sums] + 1)
                        if sums:
                            pe.wait_ge(s_adac, sums)
                        mm(bk[3][:, :], ones[:, :], acc[:, :], start=True, stop=True).then_inc(s_adam, 1)
                        sums += 1

            def three(dst, pairs):
                last = None
                for i, ((ah, al), (bh, bl)) in enumerate(pairs):
                    mm(dst, ah, bh, start=i == 0, stop=False)
                    mm(dst, ah, bl, start=False, stop=False)
                    last = mm(dst, al, bh, start=False, stop=i == len(pairs) - 1)
                return last

            pe.wait_ge(s_const, 5)
            for h in range(4):
                last = nc.tensor.transpose(bk[7][:, P * h:P * h + P], yT[:, 3, P * h:P * h + P], ident[:, :])
            last.then_inc(s_sgt, 1)
            stream("start")
            pe.wait_ge(s_sgc, 2)
            for t in range(TT):
                pe.wait_ge(s_h, t + 1)
                for hf in range(2):
                    q = 2 * t + hf
                    if q >= 4:
                        pe.wait_ge(s_tlo, q - 3)
                    for k in range(4):
                        last = nc.tensor.transpose(bk[4 + q % 4][:, P * k:P * k + P],
                                                   T[:, 2 + t % 2, P * (4 * hf + k):P * (4 * hf + k) + P], ident[:, :])
                    last.then_inc(s_tp, 1)

            def group(q):
                i, a, b = groups[q]
                u = 2 * i
                wh = lambda k: whi[:, (u + k // KU) % 3, k % KU]
                wl = lambda k: wlo[:, (u + k // KU) % 3, k % KU]
                if q == first_group[i]:
                    pe.wait_ge(s_used, split_unit[u + 1] + 1)
                if q >= 3:
                    pe.wait_ge(s_ze, q - 2)
                if a == "tok":
                    pairs = [((hTh[:, k, tok_at(b)], hTl[:, k, tok_at(b)]), (wh(k), wl(k))) for k in range(KT)]
                else:
                    c0 = slice(P * a, P * a + P)
                    pairs = [((wh(k)[:, c0], wl(k)[:, c0]), (hTh[:, k, half(b)], hTl[:, k, half(b)]))
                             for k in range(KT)]
                three(bk[q % 3][:, :], pairs).then_inc(s_z, 1)

            stream("h")
            pe.wait_ge(s_tlo, 2 * TT)
            for q in range(TT + 1):
                group(q)
            stream("mixing")
            group(TT + 1)
            group(TT + 2)
            pe.wait_ge(s_sd, 4 * N_S + 3 * TT + 2)
            pe.wait_ge(s_sgc, 2)
            V_ = yT[:, 2 * CJ + 2:2 * CJ + 4, :].rearrange("p a (t n) -> p (a t) n", n=WC)
            for h in range(4):
                mm(bk[4 + h][:, :], sgW[:, h, :], V_[:, :, 64 * h:64 * h + 64], start=True, stop=True).then_inc(s_sm, 1)
            Y = T[:, 0:2, :].rearrange("p a (t n) -> p (a t) n", n=WC)
            pe.wait_ge(s_sd, 4 * N_S + 3 * TT + 2 + 4)
            for j in range(2):
                for hf in range(2):
                    for t in range(4):
                        last = nc.tensor.transpose(bk[4 + 2 * j + hf][:, P * t:P * t + P],
                                                   Y[:, 4 * hf + t, P * j:P * j + P], ident[:, :])
                    last.then_inc(s_st, 1)

            def gates(j):
                pe.wait_ge(s_ld, N_LD * j + 3)
                if j == 0:
                    pe.wait_ge(s_se, 4)
                    pe.wait_ge(s_par, PAR_DONE)
                else:
                    pe.wait_ge(s_la, N_LA * j)
                for g in range(2):
                    for hf in range(2):
                        last = mm(bk[4 + 2 * g + hf][:, :], gateW[:, g, j, :], T[:, 1, half(hf)], start=True, stop=True)
                    last.then_inc(s_lg, 1)

            def squares(tile):
                for t in range(TT):
                    last = mm(bk[4][:, t:t + 1], T[:, tile, tok_at(t)], ones[:, 0:1], start=True, stop=True)
                last.then_inc(s_ls, 1)

            q = TT + 3
            for j in range(LJ):
                q0 = first_group[1] + 4 * j
                while q < q0 + 4:
                    group(q)
                    q += 1
                gates(j)
                if j % 2:
                    stream(f"lru{j}")
                while q < q0 + 7:
                    group(q)
                    q += 1
                pe.wait_ge(s_la, N_LA * j + 10)
                squares(3)
            for j in range(CJ):
                q0 = first_group[1 + LJ // 2 + j]
                while q < min(q0 + 9, len(groups)):
                    group(q)
                    q += 1
                pe.wait_ge(s_ca, N_CA * j + 2)
                squares(4)

            for n in range(2):
                u = 2 * (len(MIX) + n)
                pe.wait_ge(s_used, split_unit[u + 1] + 1)
                for t in range(TT):
                    i = n * TT + t
                    if i == 0:
                        pe.wait_ge(s_yl, KT)
                        pe.wait_ge(s_ze, len(groups))
                        pe.wait_ge(s_adac, len(ADA))
                        pe.wait_ge(s_ca, N_CA * CJ)
                    if i >= 2:
                        pe.wait_ge(s_od, 4 * (i - 2) + 2)
                        pe.wait_ge(s_oa, i - 1)
                    for a, (k0, k1) in enumerate(((0, CJ), (CJ, 2 * CJ), (2 * CJ, KT))):
                        three(bk[3 * (i % 2) + a][:, :],
                              [((hTh[:, k, tok_at(t)], hTl[:, k, tok_at(t)]),
                                (whi[:, (u + k // KU) % 3, k % KU], wlo[:, (u + k // KU) % 3, k % KU]))
                               for k in range(k0, k1)]).then_inc(s_o, 1)

            def logits(t):
                pe.wait_ge(s_tc2, 2 * t + 2)
                if t == 0:
                    pe.wait_ge(s_bc2, 16 * 6)
                if t >= 2:
                    pe.wait_ge(s_lgd, t - 1)
                for k in range(KT):
                    last = mm(bk[4 + t % 2][:, 0:E], h2T[t % 2][:, k, :], rw[:, k, :], start=k == 0, stop=k == KT - 1)
                last.then_inc(s_lgm, 1)

            pe.wait_ge(s_od, 8 * TT)
            for t in range(TT):
                pe.wait_ge(s_g, t + 1)
                for hf in range(2):
                    q = 2 * t + hf
                    if q >= 4:
                        pe.wait_ge(s_tc2, q - 3)
                    for k in range(4):
                        last = nc.tensor.transpose(bk[q % 4][:, P * k:P * k + P],
                                                   T[:, 2 + t % 2, P * (4 * hf + k):P * (4 * hf + k) + P], ident[:, :])
                    last.then_inc(s_tp2, 1)
                if t >= 1:
                    logits(t - 1)
            logits(TT - 1)
            pe.wait_ge(s_r, R_MASK)
            pe.wait_ge(s_rc, 9)
            for t in range(TT):
                o = bk[7][:, E * t:E * t + E]
                for s in range(t):
                    mm(o, onesb, maskb[:, s, :], start=s == 0, stop=False)
                last = mm(o, Ub, maskb[:, t, :], start=t == 0, stop=True)
            last.then_inc(s_rk, 1)
            for t in range(TT):
                last = mm(bk[7][:, TT * E:TT * E + E], onesb, maskb[:, t, :], start=t == 0, stop=t == TT - 1)
            last.then_inc(s_rk, 1)
            pe.wait_ge(s_r, R_RANK)
            pe.wait_ge(s_b2, 16)
            for t in range(TT):
                if t:
                    pe.wait_ge(s_wdc, t)
                nc.tensor.transpose(bk[7][0:E, 0:P], Wd[:, t, :], ident[:, :]).then_inc(s_wdt, 1)
                pe.wait_ge(s_wdc, t + 1)
                for n in range(2):
                    i = 2 * t + n
                    if i >= 2:
                        pe.wait_ge(s_b2c, i - 1)
                    mm(bk[5 + n][:, :], WdT[0:E, :], b2s[:, BANK * n:BANK * n + BANK], start=True, stop=True)\
                        .then_inc(s_b2m, 1)

            def x_transpose(p, blk):
                pe.wait_ge(e_gat, 32 * p + 32)
                for hf in range(2):
                    if blk:
                        pe.wait_ge(e_xtl, 4 * p + hf + 1)
                    for k in range(4):
                        last = nc.tensor.transpose(bk[4 + hf][:, P * k:P * k + P],
                                                   xg[:, blk, P * (4 * hf + k):P * (4 * hf + k) + P], ident[:, :])
                    last.then_inc(e_xtp, 1)

            pe.wait_ge(s_b2c, 2 * TT)
            x_transpose(0, 0)
            x_transpose(0, 1)

            def body(p, nb, nbn):
                inc = 3 - nb
                at = lambda i, blk: 2 * i + (blk + 1) * inc

                def products(v, blk, ah, al, ch, k0, end):
                    dst = bk[2 * (ch % 2) + blk][:, :]
                    for k in range(KU):
                        cols = slice(BANK * k, BANK * k + BANK)
                        wh, wl = unit_hi(v)[:, cols], unit_lo(v)[:, cols]
                        mm(dst, ah[:, blk, k0 + k, :], wh, start=k0 + k == 0, stop=False)
                        mm(dst, ah[:, blk, k0 + k, :], wl, start=False, stop=False)
                        last = mm(dst, al[:, blk, k0 + k, :], wh, start=False, stop=end and k == KU - 1)
                    return last

                def hidden_transpose(i):
                    for blk in range(nb):
                        pe.wait_ge(e_H, 4 * p + at(i, blk))
                        if i:
                            pe.wait_ge(e_htl, 4 * p + at(0, blk))
                        for k in range(4):
                            last = nc.tensor.transpose(bk[6 + blk][:, P * k:P * k + P],
                                                       u_sb[:, blk, P * k:P * k + P], ident[:, :])
                        last.then_inc(e_htp, inc)

                for v in range(12):
                    pe.wait_ge(*lo_count(p, v))
                    if v == 0:
                        pe.wait_ge(e_xtl, 4 * p + 4)
                    for blk in range(nb):
                        if v < 8:
                            ch, h = v // 2, v % 2
                            if h == 0 and ch < 2:
                                pe.wait_ge(e_y, 4 * p + 2 * ch + 2)
                            elif h == 0:
                                pe.wait_ge(e_t, 8 * p + at(ch - 2, blk))
                            end = products(v, blk, xTh, xTl, ch, KU * h, h == 1)
                            if h:
                                end.then_inc(e_main, inc)
                        else:
                            ch, h = (v - 8) % 2, (v - 8) // 2
                            if h == 0:
                                pe.wait_ge(e_t, 8 * p + at(2 + ch, blk))
                            pe.wait_ge(e_htl, 4 * p + at(h, blk))
                            end = products(v, blk, HTh, HTl, ch, KU * h, h == 1)
                            if h:
                                end.then_inc(e_main2, inc)
                        if h == 0 and blk == nb - 1:
                            end.then_inc(e_unit, 1)
                    if v == 5:
                        hidden_transpose(0)
                    if v == 7:
                        x_transpose(p + 1, 0)
                    if v == 8:
                        hidden_transpose(1)
                    if v == 10:
                        with pe.If(nbn == 2):
                            x_transpose(p + 1, 1)
                        with pe.If(nbn < 2):
                            pe.wait_ge(e_xtp, 4 * p + 6)
                            pe.sem_inc(e_xtp, 2)

            with pe.Fori(0, NPASS) as p:
                nb = pe.value_load(pass_tab[0:1, ds(2 * p + 1, 1)], min_val=0, max_val=2)
                nbn = pe.value_load(pass_tab[0:1, ds(2 * p + 3, 1)], min_val=0, max_val=2)
                with pe.If(nb == 2):
                    body(p, 2, nbn)
                with pe.If(nb == 1):
                    body(p, 1, nbn)


_INS = ("x", "c", "norm1_g", "norm2_g", "w_ada", "b_ada", "w_in", "conv_a_w", "sgu_w", "sgu_b", "sgu_ln_g",
        "sgu_ln_b", "conv_c_w", "conv_c_b", "rglru_gate_w", "rglru_gate_b", "rglru_lambda", "mix_norm_g",
        "w_out", "router_w", "router_b", "expert_w1", "expert_b1", "expert_w2", "expert_b2", "final_norm_g")
_OUTS = [((1, 1024, 1024), "float32")]


def kernel(**inputs):
    import numpy as _np
    import concourse.bacc as _bacc
    from concourse import mybir as _mybir
    from concourse.bass_utils import run_bass_kernel_spmd as _run

    nc = _bacc.Bacc("TRN2", target_bir_lowering=False, num_devices=1)
    arrays, args = {}, []
    for name in _INS:
        a = _np.ascontiguousarray(inputs[name])
        arrays[f"in_{name}_dram"] = a
        args.append(nc.dram_tensor(f"in_{name}_dram", a.shape, _mybir.dt.from_np(a.dtype), kind="ExternalInput").ap())
    for i, (shape, dtype) in enumerate(_OUTS):
        dt = _mybir.dt.from_np(_np.dtype(dtype))
        args.append(nc.dram_tensor(f"out_{i}_dram", shape, dt, kind="ExternalOutput").ap())
    decoder_kernel(nc, *args)
    r = _run(nc, [arrays], core_ids=[0])
    got = tuple(r.results[0][f"out_{i}_dram"] for i in range(len(_OUTS)))
    return got[0]
```

```python
import concourse.bass as bass
from concourse import mybir
from contextlib import ExitStack

P = 128
BANK = 512


def decoder_kernel(nc, x, c, norm1_g, norm2_g, w_ada, b_ada, w_in, conv_a_w, sgu_w, sgu_b, sgu_ln_g,
                   sgu_ln_b, conv_c_w, conv_c_b, gate_w, gate_b, lam, mix_g, w_out, router_w,
                   router_b, w1, b1, w2, b2, final_g, out):
    f32, f32r, bf16 = mybir.dt.float32, mybir.dt.float32r, mybir.dt.bfloat16
    i32, u32 = mybir.dt.int32, mybir.dt.uint32
    ALU, ACT, AX = mybir.AluOpType, mybir.ActivationFunctionType, mybir.AxisListType
    ds = bass.ds

    SEQ, D = x.shape[1], x.shape[2]
    TT, KT = SEQ // P, D // P
    E = router_w.shape[2]
    TOPK = 4
    FF = w2.shape[2]
    WC = conv_a_w.shape[2]
    WL = conv_c_w.shape[2]
    LJ, CJ = WL // P, WC // P
    NMOD = 6
    EPS = 1e-6
    LIMIT, ALPHA = 7.0, 1.702
    GELU_C, GELU_A = 0.7978845608028654, 0.044715
    PASS = 2 * P
    NPASS = E + SEQ * TOPK // PASS
    GROUP = 4
    assert NPASS % GROUP == 0
    NBLK = 2 * (NPASS + 1)
    KU = KT // 2
    UNIT = KU * BANK
    PADROW = SEQ

    mod_d = nc.dram_tensor("mod_d", (NMOD * D,), f32, kind="Internal").ap()
    x1_d = nc.dram_tensor("x1_d", (SEQ, D), f32, kind="Internal").ap()
    h2_d = nc.dram_tensor("h2_d", (SEQ + P, D), f32, kind="Internal").ap()
    acc_d = nc.dram_tensor("acc_d", (SEQ + P, D), f32, kind="Internal").ap()
    spare_d = nc.dram_tensor("spare_d", (SEQ + P, 2), f32, kind="Internal").ap()
    zero_d = nc.dram_tensor("zero_d", (SEQ + P, 2), f32, kind="Internal").ap()
    slot_d = nc.dram_tensor("slot_d", (P * NBLK, 2), i32, kind="Internal").ap()
    pass_d = nc.dram_tensor("pass_d", (P, 2), i32, kind="Internal").ap()

    xf = x[0]
    outf = out[0]

    ctx = ExitStack()
    with ctx:
        def sb(name, shape, dt, where=ctx):
            return where.enter_context(nc.sbuf_tensor(name, shape, dt))

        def sem(name):
            return ctx.enter_context(nc.semaphore(name))

        rawA = sb("rawA", [P, 3, UNIT], f32)
        whi = sb("whi", [P, 3, KU, BANK], f32r)
        wlo = sb("wlo", [P, 3, KU, BANK], f32r)
        ident = sb("ident", [P, P], f32)
        idx_tab = sb("idx_tab", [P, NBLK], u32)
        wgt_tab = sb("wgt_tab", [P, NBLK], f32)
        pass_tab = sb("pass_tab", [1, NBLK], i32)
        tiny = sb("tiny", [P, 3], f32)
        idx_g = sb("idx_g", [P, 2], u32)
        idx_s = sb("idx_s", [P, 2], u32)
        wcur = sb("wcur", [P, 2], f32)
        xpad = sb("xpad", [P, 2], f32)
        mhalf = sb("mhalf", [P, TT], f32)

        front = ExitStack()
        hTh = sb("hTh", [P, KT, SEQ], f32r, front)
        hTl = sb("hTl", [P, KT, SEQ], f32r, front)
        yT = sb("yT", [P, KT, SEQ], f32, front)
        T = sb("T", [P, 5, SEQ], f32, front)
        ones = sb("ones", [P, P], f32, front)
        ccol = sb("ccol", [P, KT], f32, front)
        gateW = sb("gateW", [P, 2, LJ, P], f32, front)
        gateB = sb("gateB", [P, 2, LJ], f32, front)
        gateBh = sb("gateBh", [P, 2, LJ], f32, front)
        lamc = sb("lamc", [P, LJ], f32, front)
        sp = sb("sp", [P, 6, LJ], f32, front)
        cw = sb("cw", [P, 4, LJ], f32, front)
        cb = sb("cb", [P, LJ], f32, front)
        caw = sb("caw", [P, 3, CJ], f32, front)
        mixg = sb("mixg", [P, KT], f32, front)
        sgW = sb("sgW", [P, 4, P], f32, front)
        sgB = sb("sgB", [P, 4], f32, front)
        acc = sb("acc", [P, 2, BANK], f32, front)
        brows = sb("brows", [NMOD * D // BANK, BANK], f32, front)
        ss = sb("ss", [P, TT], f32, front)
        rs = sb("rs", [P, TT], f32, front)
        bnst = sb("bnst", [P, TT, 6], f32, front)
        mv = sb("mv", [P, TT, 2], f32, front)
        ssq = sb("ssq", [P, KT, TT], f32, front)
        rg = sb("rg", [P, 3, TT], f32, front)
        modrow = sb("modrow", [1, 2, BANK], f32, front)

        flat = yT[:, :, :].rearrange("p k s -> p (k s)")
        tail0 = 3 * SEQ

        def carve(n, dt=f32):
            nonlocal tail0
            a = flat[:, tail0:tail0 + n]
            tail0 += n
            return a if dt == f32 else a.bitcast(dt)

        rw = carve(KT * E).rearrange("p (k e) -> p k e", e=E)
        rb = carve(E)
        h2T = [carve(D).rearrange("p (k s) -> p k s", s=P) for _ in range(2)]
        lg = carve(TT * E).rearrange("p (t e) -> p t e", e=E)
        v8 = carve(TT * 8).rearrange("p (t k) -> p t k", k=8)
        i8 = carve(TT * 8, u32).rearrange("p (t k) -> p t k", k=8)
        i8f = carve(TT * TOPK).rearrange("p (t k) -> p t k", k=TOPK)
        dv = carve(TT * TOPK).rearrange("p (t k) -> p t k", k=TOPK)
        w4 = carve(TT * TOPK).rearrange("p (t k) -> p t k", k=TOPK)
        sm = carve(TT)
        rsm = carve(TT)
        iotaE = carve(E)
        iotaEi = carve(E, i32)
        mask = carve(TT * E).rearrange("p (t e) -> p t e", e=E)
        maskb = carve(TT * E // 2, bf16).rearrange("p (t e) -> p t e", e=E)
        Ub = carve(P // 2, bf16)
        onesb = carve(P // 2, bf16)
        cnt = carve(E)
        npe = carve(E)
        tmpe = carve(E)
        onee = carve(E)
        endp = carve(E)
        begp = carve(E)
        slot = carve(TT * E).rearrange("p (t e) -> p t e", e=E)
        slf = carve(TT * TOPK)
        sli = carve(TT * TOPK, i32)
        blki = carve(TT * TOPK, i32)
        remi = carve(TT * TOPK, i32)
        loci = carve(TT * TOPK, i32)
        pair = carve(TT * TOPK * 2, i32).rearrange("p (n c) -> p n c", c=2)
        tok = carve(TT, i32)
        pidi = carve(1, i32)
        pid = carve(1)
        pm = carve(4 * E).rearrange("p (a e) -> p a e", e=E)
        pcol = carve(4)
        pcoli = carve(2, i32)
        WdT = carve(P)
        assert tail0 <= KT * SEQ
        OH = T[:, 3, :].rearrange("p (n e) -> p n e", e=E)
        WOH = T[:, 4, :].rearrange("p (n e) -> p n e", e=E)
        Wd = T[:, 2, 0:TT * E].rearrange("p (t e) -> p t e", e=E)
        init_tab = T[:, 2, 512:512 + 2 * NBLK].bitcast(i32).rearrange("p (b c) -> p b c", c=2)
        b2s = T[0:E, 0, :]
        stage = T[:, 4, :].rearrange("p (a n) -> p a n", a=2)
        lng = yT[:, 2, 0:2 * WC].rearrange("p (a n) -> p a n", a=2)

        x_slot = lambda t: T[:, 0, :] if t == 4 else yT[:, (4 + t if t < 4 else t - 1), :]
        Z_AT = (T[:, 1, :], T[:, 0, :], T[:, 2, :], T[:, 1, :])
        W_AT = (yT[:, 3, :], T[:, 4, :], T[:, 3, :], yT[:, 3, :])

        Y2 = (2, 2, 2, 4)

        front.close()

        held = ExitStack()
        rawB = sb("rawB", [P, 3, UNIT], f32, held)
        whi3 = sb("whi3", [P, KU, BANK], f32r, held)
        wlo3 = sb("wlo3", [P, KU, BANK], f32r, held)
        b1s = sb("b1s", [P, 2, BANK], f32, held)
        back = ExitStack()
        xg = sb("xg", [P, 2, D], f32, back)
        xTh = sb("xTh", [P, 2, KT, P], f32r, back)
        xTl = sb("xTl", [P, 2, KT, P], f32r, back)
        HTh = sb("HTh", [P, 2, KT, P], f32r, back)
        HTl = sb("HTl", [P, 2, KT, P], f32r, back)
        g_sb = sb("g_sb", [P, 2, BANK], f32, back)
        u_sb = sb("u_sb", [P, 2, BANK], f32, back)
        th = sb("th", [P, 2, BANK], f32, back)
        y_sb = sb("y_sb", [P, 2, D], f32, back)
        back.close()
        last = ExitStack()
        fx = sb("fx", [P, TT, D], f32, last)
        fa = sb("fa", [P, TT, D], f32, last)
        fsq = sb("fsq", [P, D], f32, last)
        fmod = sb("fmod", [P, 2, D], f32, last)
        fss = sb("fss", [P, TT], f32, last)
        frs = sb("frs", [P, TT], f32, last)
        last.close()
        held.close()

        bk = [ctx.enter_context(nc.psum_tensor(f"bank{i}", [P, BANK], f32)) for i in range(8)]

        s_const = sem("s_const")
        s_small = sem("s_small")
        s_raw = [sem(f"s_raw{i}") for i in range(3)]
        s_ccol = sem("s_ccol")
        s_brows = sem("s_brows")
        s_used = sem("s_used")
        s_usede = sem("s_usede")
        s_adap = sem("s_adap")
        s_adam = sem("s_adam")
        s_adac = sem("s_adac")
        s_adad = [sem("s_adad0"), sem("s_adad1")]
        s_bc = sem("s_bc")
        s_A = sem("s_A")
        s_x = [sem(f"s_x{i}") for i in range(5)]
        s_sq = sem("s_sq")
        s_rp = sem("s_rp")
        s_h0 = sem("s_h0")
        s_h = sem("s_h")
        s_tp = sem("s_tp")
        s_thi = sem("s_thi")
        s_tlo = sem("s_tlo")
        s_hi = sem("s_hi")
        s_z = sem("s_z")
        s_ze = sem("s_ze")
        s_par = sem("s_par")
        s_lng = sem("s_lng")
        s_sgt = sem("s_sgt")
        s_sgc = sem("s_sgc")
        s_sa = sem("s_sa")
        s_sd = sem("s_sd")
        s_sp = sem("s_sp")
        s_sm = sem("s_sm")
        s_st = sem("s_st")
        s_se = sem("s_se")
        s_la = sem("s_la")
        s_ld = sem("s_ld")
        s_lg = sem("s_lg")
        s_sy = sem("s_sy")
        s_ss = sem("s_ss")
        s_ls = sem("s_ls")
        s_ca = sem("s_ca")
        s_cd = sem("s_cd")
        s_rg = sem("s_rg")
        s_rgp = sem("s_rgp")
        s_yh = sem("s_yh")
        s_yl = sem("s_yl")
        s_o = sem("s_o")
        s_oa = sem("s_oa")
        s_od = sem("s_od")
        s_xo = [sem("s_xo0"), sem("s_xo1")]
        s_x1 = [sem("s_x10"), sem("s_x11")]
        s_gate1 = sem("s_gate1")
        s_bc2 = sem("s_bc2")
        s_A2 = sem("s_A2")
        s_x2 = [sem("s_x20"), sem("s_x21")]
        s_sq2 = sem("s_sq2")
        s_rp2 = sem("s_rp2")
        s_g0 = sem("s_g0")
        s_g = sem("s_g")
        s_h2d = [sem("s_h2d0"), sem("s_h2d1")]
        s_pad = sem("s_pad")
        s_tp2 = sem("s_tp2")
        s_tc2 = sem("s_tc2")
        s_lgm = sem("s_lgm")
        s_lgd = sem("s_lgd")
        s_r = sem("s_r")
        s_re = sem("s_re")
        s_rc = sem("s_rc")
        s_rk = sem("s_rk")
        s_wdt = sem("s_wdt")
        s_wdc = sem("s_wdc")
        s_b2 = sem("s_b2")
        s_b2m = sem("s_b2m")
        s_b2c = sem("s_b2c")
        s_b2d = [sem("s_b2d0"), sem("s_b2d1")]
        s_tab0 = sem("s_tab0")
        s_scat = sem("s_scat")
        s_tab = sem("s_tab")
        s_pt = sem("s_pt")
        s_ptl = sem("s_ptl")
        s_tabc = sem("s_tabc")
        e_raw = [sem(f"e_raw{i}") for i in range(6)]
        e_hi = sem("e_hi")
        e_lo = sem("e_lo")
        e_lop = sem("e_lop")
        e_unit = sem("e_unit")
        e_b1 = [sem("e_b10"), sem("e_b11")]
        e_main = sem("e_main")
        e_t = sem("e_t")
        e_g = sem("e_g")
        e_u = sem("e_u")
        e_th = sem("e_th")
        e_gs = sem("e_gs")
        e_H = sem("e_H")
        e_htp = sem("e_htp")
        e_hth = sem("e_hth")
        e_htl = sem("e_htl")
        e_xtp = sem("e_xtp")
        e_xth = sem("e_xth")
        e_xtl = sem("e_xtl")
        e_main2 = sem("e_main2")
        e_y = sem("e_y")
        e_idx = sem("e_idx")
        e_w = sem("e_w")
        e_gat = sem("e_gat")
        e_scat = sem("e_scat")
        e_free = sem("e_free")
        e_go = sem("e_go")
        f_bc = sem("f_bc")
        f_x = [sem(f"f_x{t}") for t in range(TT)]
        f_d = sem("f_d")
        f_e = sem("f_e")
        f_a = sem("f_a")
        f_p = sem("f_p")
        f_o = sem("f_o")
        e_end = sem("e_end")

        SMALL = 16 * 18
        N_S, N_LD, N_LA, N_CD, N_CA = 5, 11, 10, 4, 2
        R_MASK, R_WD, R_RANK, R_SLOT, R_PASS = 7, 12, 24, 33, 44
        POOL_UNITS = (5, 10)
        TERMS = 9
        PAR_DONE = 2 + 5 + (TERMS - 1) + 6
        ZEROED = 3

        MIX = ["S"] + [("L", j) for j in range(LJ // 2)] + [("C", j) for j in range(CJ)]
        ada = lambda a, b: [("ada", n, h) for n in range(a, b) for h in range(2)]
        mix = lambda i: [("mix", i, h) for h in range(2)]
        order = ada(0, 3) + mix(0) + ada(3, 4) + mix(1) + ada(4, 6) + mix(2) + ada(6, 9) + mix(3) + ada(9, 12) + mix(4)
        assert len(MIX) == 5 and NMOD * D // BANK == 12
        order += [("out", n, h) for n in range(2) for h in range(2)]
        split = [u for u in order if u[0] != "ada"]
        NF = len(order)
        ADA = [n for k, n, h in order if k == "ada" and h == 0]
        NOW = 4
        on_pe = lambda i: i % 2 == 1 or i >= NOW
        freed = []
        for k, n, h in order:
            on = s_usede if k == "ada" and on_pe(n) else s_used
            freed.append((on, 1 + sum(f[0] is on for f in freed)))
        USED = sum(f[0] is s_used for f in freed)

        def columns(i):
            m = MIX[i]
            if m == "S":
                return [(3 * WC, 2 * WC)]
            base = 3 * WC + 2 * WC
            if m[0] == "L":
                return [(base + WL + 2 * P * m[1], 2 * P), (base + 2 * P * m[1], 2 * P)]
            return [(WC * a + P * m[1], P) for a in range(3)]

        def raw_count(u):
            return 16 * sum(dmas(order[v]) for v in range(u % 3, u + 1, 3))

        def dmas(unit):
            return len(columns(unit[1])) if unit[0] == "mix" else 1

        POINTS = {"start": ["a"] * 3 + [0, 1] + ["a"], "h": [2], "gating": [3], "mixing": ["a"] * 2,
                  "lru0": [4], "lru1": [5, "a"], "lru2": ["a"] * 2, "lru3": [6, 7, "a"],
                  "conv0": ["a"] * 2 + [8, 9, 10], "conv1": [11, 12], "out0": [13]}

        groups = []
        for i, m in enumerate(MIX):
            if m == "S":
                groups += [(i, "tok", t) for t in range(TT)]
            elif m[0] == "L":
                groups += [(i, a + jj, hf) for jj in range(2) for a in (0, 2) for hf in range(2)]
            else:
                groups += [(i, a, hf) for a in range(3) for hf in range(2)]
        first_group = [next(q for q, g in enumerate(groups) if g[0] == i) for i in range(len(MIX))]
        first_group.append(len(groups))
        HS = SEQ // 2

        def store_x1(eng, i):
            n, t = divmod(i, TT)
            eng.wait_ge(s_od, 4 * i + 4)
            eng.dma_start(x1_d[P * t:P * t + P, BANK * n:BANK * n + BANK], T[:, i % 2, BANK:2 * BANK])\
               .then_inc(s_x1[i % 2], 16)

        def store_h2(eng, t):
            eng.wait_ge(s_g, t + 1)
            eng.dma_start(h2_d[P * t:P * t + P, :], T[:, 2 + t % 2, :]).then_inc(s_h2d[t % 2], 16)

        def scatter(pool, blk):
            pool.indirect_dma_start(acc_d, bass.IndirectOffsetOnAxis(ap=idx_s[:, blk:blk + 1], axis=0),
                                    y_sb[:, blk, :], None, compute_op=ALU.add).then_inc(e_scat, 16)

        def raw5(p, v):
            return 32 * p + 16 * (v // 6 + 1)

        def lo_count(p, v):
            if v % 12 in POOL_UNITS:
                return e_lop, len(POOL_UNITS) * p + (len(POOL_UNITS) * (v // 12) + POOL_UNITS.index(v % 12) + 1)
            before = sum(w % 12 not in POOL_UNITS for w in range(v + 1))
            return e_lo, (12 - len(POOL_UNITS)) * p + before

        def unit_hi(v):
            return (whi[:, v % 4] if v % 4 < 3 else whi3[:, :, :]).rearrange("p k n -> p (k n)")

        def unit_lo(v):
            return (wlo[:, v % 4] if v % 4 < 3 else wlo3[:, :, :]).rearrange("p k n -> p (k n)")

        ctx.enter_context(nc.allow_non_contiguous_dma(reason="small parameters, channels on partitions"))
        block = ctx.enter_context(nc.Block())

        @block.sync
        def _(eng):
            small = 0

            def load(dst, src):
                nonlocal small
                eng.dma_start(dst, src).then_inc(s_small, 16)
                small += 16

            def unit(u):
                kind, n, h = order[u]
                if u >= 3:
                    eng.wait_ge(*freed[u - 3])
                dst = rawA[:, u % 3, :].rearrange("p (k n) -> p k n", n=BANK)
                if kind == "mix":
                    at = 0
                    for s0, wd in columns(n):
                        src = w_in[0].rearrange("(k p) n -> p k n", p=P)[:, KU * h:KU * h + KU, s0:s0 + wd]
                        eng.dma_start(dst[:, :, at:at + wd], src).then_inc(s_raw[u % 3], 16)
                        at += wd
                else:
                    w = (w_ada if kind == "ada" else w_out)[0].rearrange("(k p) n -> p k n", p=P)
                    eng.dma_start(dst, w[:, KU * h:KU * h + KU, BANK * n:BANK * n + BANK])\
                       .then_inc(s_raw[u % 3], 16)

            def x_tile(t):
                if t >= 5:
                    eng.wait_ge(s_h0, t - 4)
                    eng.wait_ge(s_sq, t - 4)
                eng.dma_start(x_slot(t), xf[P * t:P * t + P, :]).then_inc(s_x[t % 5], 16)

            eng.dma_start(ccol[:, :], c[0].rearrange("(k p) -> p k", p=P)).then_inc(s_ccol, 16)
            for u in range(3):
                unit(u)
            eng.dma_start(brows[:, :], b_ada[0].rearrange("(i n) -> i n", n=BANK)).then_inc(s_brows, 16)
            x_tile(0)
            x_tile(1)
            for u in range(3, 6):
                unit(u)
                x_tile(u - 1)
            eng.dma_start(yT[:, 2, :], norm1_g[0:1, :].to_broadcast([P, D])).then_inc(s_bc, 16)
            for u in range(6, 10):
                unit(u)
            for d in range(2):
                for g in range(2):
                    load(gateW[64 * d:64 * d + 64, g, :, 64 * d:64 * d + 64],
                         gate_w[0, g].rearrange("(j a) i q -> i a j q", a=2)[:, d])
            for g in range(2):
                load(gateB[:, g, :], gate_b[0, g].rearrange("(j a) q -> (a q) j", a=2))
            load(lamc[:, :], lam[0].rearrange("(j p) -> p j", p=P))
            for k in range(4):
                load(cw[:, k, :], conv_c_w[0, k].rearrange("(j p) -> p j", p=P))
            load(cb[:, :], conv_c_b[0].rearrange("(j p) -> p j", p=P))
            for k in range(3):
                load(caw[:, k, :], conv_a_w[0, k].rearrange("(j p) -> p j", p=P))
            load(mixg[:, :], mix_g[0].rearrange("(j p) -> p j", p=P))
            load(sgB[:, :], sgu_b[0].rearrange("h t -> t h"))
            load(sgW[:, :, :], sgu_w[0].rearrange("h t s -> t h s"))
            assert small == SMALL
            for t in range(5, TT):
                x_tile(t)
            eng.wait_ge(s_A, 1)
            eng.dma_start(lng[:, 0, :], sgu_ln_g[0:1, :].to_broadcast([P, WC])).then_inc(s_lng, 16)
            eng.dma_start(lng[:, 1, :], sgu_ln_b[0:1, :].to_broadcast([P, WC])).then_inc(s_lng, 16)
            for u in range(10, NF):
                unit(u)
            eng.wait_ge(s_yl, KT)
            eng.wait_ge(s_ls, LJ + CJ)
            for i in range(2):
                eng.wait_ge(s_adad[i], 16 * ((len(ADA) - NOW) // 2))
            eng.dma_start(T[:, 4, :], mod_d[2 * D:3 * D].rearrange("(a n) -> a n", a=1).to_broadcast([P, D]))\
               .then_inc(s_gate1, 16)
            for n in range(2):
                for t in range(TT):
                    i = n * TT + t
                    if i >= 2:
                        eng.wait_ge(s_od, 4 * (i - 2) + 4)
                        eng.wait_ge(s_x1[i % 2], 16 * (i // 2))
                    eng.dma_start(T[:, 2 + i % 2, 0:BANK], xf[P * t:P * t + P, BANK * n:BANK * n + BANK])\
                       .then_inc(s_xo[i % 2], 16)
                    if i >= 1:
                        store_x1(eng, i - 1)
                    if i == 3:
                        for a, src in enumerate((mod_d[3 * D:4 * D].rearrange("(a n) -> a n", a=1),
                                                 mod_d[4 * D:5 * D].rearrange("(a n) -> a n", a=1), norm2_g[0:1, :])):
                            eng.dma_start(yT[:, a, :], src.to_broadcast([P, D])).then_inc(s_bc2, 16)
                        eng.dma_start(rw, router_w[0].rearrange("(k p) e -> p k e", p=P)).then_inc(s_bc2, 16)
                        eng.dma_start(rb, router_b[0:1, :].to_broadcast([P, E])).then_inc(s_bc2, 16)
            store_x1(eng, 2 * TT - 1)
            for t in range(TT):
                if t < 2:
                    eng.wait_ge(s_x1[t], 16 * TT)
                if t >= 2:
                    eng.wait_ge(s_g0, t - 1)
                    eng.wait_ge(s_sq2, t - 1)
                eng.dma_start(T[:, t % 2, :], x1_d[P * t:P * t + P, :]).then_inc(s_x2[t % 2], 16)
                if t >= 1:
                    store_h2(eng, t - 1)
            store_h2(eng, TT - 1)
            def w_unit(e, v):
                dst = (rawA if v % 6 < 3 else rawB)[:, v % 3, :].rearrange("p (k n) -> p k n", n=BANK)
                if v < 8:
                    ch, h = v // 2, v % 2
                    col = (ch % 2) * FF + (ch // 2) * BANK
                    w = w1[0, ds(e, 1)]
                else:
                    ch, h = (v - 8) % 2, (v - 8) // 2
                    col = ch * BANK
                    w = w2[0, ds(e, 1)]
                src = w.rearrange("a (k p) n -> p (a k) n", p=P)[:, KU * h:KU * h + KU, col:col + BANK]
                eng.dma_start(dst, src).then_inc(e_raw[v % 6], 16)

            def b1_chunk(e, ch):
                col = (ch % 2) * FF + (ch // 2) * BANK
                eng.dma_start(b1s[:, ch % 2, :], b1[0, ds(e, 1), col:col + BANK].to_broadcast([P, BANK]))\
                   .then_inc(e_b1[ch % 2], 16)

            eng.wait_ge(s_used, USED)
            eng.wait_ge(s_o, 6 * TT)
            for v in range(6):
                w_unit(0, v)
            for ch in range(2):
                b1_chunk(0, ch)
            eng.wait_ge(s_g0, TT)
            eng.wait_ge(s_h2d[0], 16 * (TT // 2))
            eng.wait_ge(s_h2d[1], 16 * (TT // 2))
            eng.wait_ge(s_rc, ZEROED)
            eng.dma_start(h2_d[SEQ:SEQ + P, :], T[:, 1, :]).then_inc(s_pad, 16)
            eng.dma_start(acc_d[SEQ:SEQ + P, :], T[:, 1, :]).then_inc(s_pad, 16)
            eng.dma_start(zero_d.rearrange("(p c) b -> p (c b)", p=P), T[:, 1, 0:2 * (SEQ + P) // P]).then_inc(s_pad, 16)
            eng.dma_start(slot_d.rearrange("(p b) c -> p b c", p=P), init_tab).then_inc(s_tab0, 16)
            eng.dma_start(b2s, b2[0]).then_inc(s_b2, 16)
            eng.wait_ge(s_r, R_PASS)
            eng.dma_start(pass_d, pcoli).then_inc(s_pt, 16)
            eng.wait_ge(s_pt, 16)
            eng.dma_start(pass_tab[0:1, :], pass_d[0:NPASS + 1, :].rearrange("p c -> (p c)").rearrange("(a n) -> a n", a=1))\
               .then_inc(s_ptl, 16)
            eng.wait_ge(s_scat, 16 * TT * TOPK)
            eng.dma_start(T[:, 3, 0:2 * NBLK].bitcast(i32).rearrange("p (b c) -> p b c", c=2),
                          slot_d.rearrange("(p b) c -> p b c", p=P)).then_inc(s_tab, 16)

            eng.wait_ge(s_ptl, 16)
            with eng.Fori(0, NPASS // GROUP) as g:
                live = eng.value_load(pass_tab[0:1, ds(2 * GROUP * g + 1, 1)], min_val=0, max_val=2)
                with eng.If(live > 0):
                    with eng.Fori(0, GROUP) as i:
                        p = GROUP * g + i
                        nb = eng.value_load(pass_tab[0:1, ds(2 * p + 1, 1)], min_val=0, max_val=2)
                        with eng.If(nb > 0):
                            ex = eng.value_load(pass_tab[0:1, ds(2 * p, 1)], min_val=0, max_val=E - 1)
                            en = eng.value_load(pass_tab[0:1, ds(2 * p + 2, 1)], min_val=0, max_val=E - 1)
                            for w in range(6, 18):
                                eng.wait_ge(*lo_count(p, w - 6))
                                w_unit(ex if w < 12 else en, w % 12)
                                if w in (7, 9):
                                    ch = (w - 3) // 2
                                    eng.wait_ge(e_t, 8 * p + 2 * (ch - 2) + 2)
                                    b1_chunk(ex, ch)
                                if w in (11, 13):
                                    ch = (w - 11) // 2
                                    eng.wait_ge(e_t, 8 * p + 2 * (ch + 2) + 2)
                                    b1_chunk(en, ch)
            eng.wait_ge(e_end, 3)
            for t in range(TT):
                eng.dma_start(fa[:, t, :], acc_d[P * t:P * t + P, :]).then_inc(f_x[t], 16)
                if t == 0:
                    eng.dma_start(fmod[:, 0, :], mod_d[5 * D:6 * D].rearrange("(a n) -> a n", a=1).to_broadcast([P, D]))\
                       .then_inc(f_bc, 16)
                eng.dma_start(fx[:, t, :], x1_d[P * t:P * t + P, :]).then_inc(f_x[t], 16)
                if t == 0:
                    eng.dma_start(fmod[:, 1, :], final_g.rearrange("(a n) -> a n", a=1).to_broadcast([P, D]))\
                       .then_inc(f_bc, 16)
            for t in range(TT):
                eng.wait_ge(f_e, t + 1)
                eng.dma_start(outf[P * t:P * t + P, :], fa[:, t, :]).then_inc(f_o, 16)
            eng.wait_ge(f_o, 16 * TT)

        @block.gpsimd
        def _(pool):
            pool.memset(ident[:, :], 0.0).then_inc(s_const, 1)
            pool.memset(ones[:, :], 1.0).then_inc(s_const, 1)
            pool.memset(mhalf[:, :], -0.5).then_inc(s_const, 1)
            pool.wait_ge(s_const, 3)
            pool.affine_select(out=ident[:, :], in_=ident[:, :], compare_op=ALU.not_equal, fill=1.0,
                               base=0, pattern=[[-1, P]], channel_multiplier=1).then_inc(s_const, 1)
            def power(dst, src, scale, done, step, n, e=1):
                pool.tensor_scalar(dst, src, scale, EPS, ALU.mult, ALU.add).then_inc(done, 1)
                pool.wait_ge(done, step + 1)
                pool.tensor_tensor(dst, dst, mhalf[:, 0:n], ALU.pow).then_inc(done, 1)

            for t in range(5):
                pool.wait_ge(s_sq, t + 1)
                power(rs[:, t:t + 1], ss[:, t:t + 1], 1.0 / D, s_rp, 2 * t, 1)
            pool.wait_ge(s_small, SMALL)
            pool.affine_select(out=sgW[:, :, :], in_=sgW[:, :, :], compare_op=ALU.is_ge, fill=0.0, base=0,
                               pattern=[[0, 4], [-1, P]], channel_multiplier=1).then_inc(s_const, 1)
            for t in range(5, TT):
                pool.wait_ge(s_sq, t + 1)
                power(rs[:, t:t + 1], ss[:, t:t + 1], 1.0 / D, s_rp, 2 * t, 1)
            pool.wait_ge(s_sd, 4 * N_S + 2 * TT)
            pool.wait_ge(s_h0, TT)
            power(rs[:, :], mv[:, :, 1], 1.0, s_sp, 0, TT)
            pool.wait_ge(s_rg, 4)
            power(rg[:, 0, :], rg[:, 0, :], 1.0 / WC, s_rgp, 0, TT)
            power(rg[:, 1, :], ssq[:, 2, :], 1.0 / WC, s_rgp, 2, TT)
            power(rg[:, 2, :], rg[:, 2, :], 1.0 / WL, s_rgp, 4, TT)

            for t in range(TT):
                pool.wait_ge(s_sq2, t + 1)
                power(rs[:, t:t + 1], ss[:, t:t + 1], 1.0 / D, s_rp2, 2 * t, 1)
            pool.wait_ge(s_g0, TT)
            pool.wait_ge(s_h2d[0], 16 * (TT // 2))
            pool.wait_ge(s_tp2, 2 * TT)
            pool.memset(T[:, 1, :], 0.0).then_inc(s_rc, 1)
            pool.memset(init_tab[:, :, 1], 0).then_inc(s_rc, 1)
            pool.iota(init_tab[:, :, 0], pattern=[[0, NBLK]], base=PADROW, channel_multiplier=1).then_inc(s_rc, 1)
            pool.iota(iotaEi, pattern=[[1, E]], base=0, channel_multiplier=0).then_inc(s_rc, 1)
            pool.iota(tok, pattern=[[P, TT]], base=0, channel_multiplier=1).then_inc(s_rc, 1)
            pool.iota(pidi, pattern=[[0, 1]], base=0, channel_multiplier=1).then_inc(s_rc, 1)
            pool.memset(onesb, 1.0).then_inc(s_rc, 1)
            pool.memset(onee, 1.0).then_inc(s_rc, 1)
            pool.wait_ge(s_rc, 8)
            pool.affine_select(out=Ub, in_=onesb, compare_op=ALU.is_gt, fill=0.0, base=0,
                               pattern=[[1, P]], channel_multiplier=-1).then_inc(s_rc, 1)
            pool.wait_ge(s_r, R_SLOT)
            pool.wait_ge(s_tab0, 16)
            for n in range(TT * TOPK):
                pool.indirect_dma_start(slot_d, bass.IndirectOffsetOnAxis(ap=loci[:, n:n + 1].bitcast(u32), axis=0),
                                        pair[:, n, :], None).then_inc(s_scat, 16)

            def gather(blk):
                pool.indirect_dma_start(xg[:, blk, :], None, h2_d,
                                        bass.IndirectOffsetOnAxis(ap=idx_g[:, blk:blk + 1], axis=0))\
                    .then_inc(e_gat, 16)

            def lo(p, v):
                pool.wait_ge(e_hi, 12 * p + v + 1)
                pool.tensor_tensor(unit_lo(v), (rawA if v % 6 < 3 else rawB)[:, v % 3, :], unit_hi(v).bitcast(f32),
                                   ALU.subtract).then_inc(e_lop, 1)

            pool.wait_ge(s_tabc, 2)
            pool.wait_ge(s_pad, 48)
            pool.tensor_copy(idx_g[:, :], idx_tab[:, 0:2]).then_inc(e_idx, 1)
            pool.wait_ge(e_idx, 1)
            gather(0)
            gather(1)
            for i in range(2):
                if i:
                    pool.wait_ge(e_scat, 16)
                pool.indirect_dma_start(spare_d, bass.IndirectOffsetOnAxis(ap=idx_tab[:, NBLK - 1:NBLK], axis=0),
                                        wgt_tab[:, NBLK - 2:NBLK], None).then_inc(e_scat, 16)
            pool.wait_ge(e_scat, 32)
            pool.wait_ge(s_b2d[0], 16 * TT)
            pool.wait_ge(s_b2d[1], 16 * TT)
            pool.wait_ge(s_ptl, 16)
            with pool.Fori(0, NPASS // GROUP) as g:
                live = pool.value_load(pass_tab[0:1, ds(2 * GROUP * g + 1, 1)], min_val=0, max_val=2)
                with pool.If(live > 0):
                    with pool.Fori(0, GROUP) as i:
                        p = GROUP * g + i
                        nb = pool.value_load(pass_tab[0:1, ds(2 * p + 1, 1)], min_val=0, max_val=2)
                        with pool.If(nb > 0):
                            nbn = pool.value_load(pass_tab[0:1, ds(2 * p + 3, 1)], min_val=0, max_val=2)
                            pool.wait_ge(e_xtp, 4 * p + 4)
                            pool.wait_ge(e_gat, 32 * p + 32)
                            pool.tensor_copy(idx_g[:, :], idx_tab[:, ds(2 * p + 2, 2)]).then_inc(e_idx, 1)
                            pool.wait_ge(e_idx, p + 2)
                            pool.sem_inc(e_go, 1)
                            gather(0)
                            with pool.If(nbn == 2):
                                gather(1)
                            with pool.If(nbn < 2):
                                pool.indirect_dma_start(xpad[:, :], None, zero_d,
                                                        bass.IndirectOffsetOnAxis(ap=idx_g[:, 1:2], axis=0))\
                                    .then_inc(e_gat, 16)
                            lo(p, POOL_UNITS[0])
                            pool.wait_ge(e_scat, 32 * p + 32)
                            pool.sem_inc(e_free, 1)
                            pool.tensor_copy(idx_s[:, :], idx_tab[:, ds(2 * p, 2)]).then_inc(e_w, 1)
                            pool.tensor_copy(wcur[:, :], wgt_tab[:, ds(2 * p, 2)]).then_inc(e_w, 1)
                            lo(p, POOL_UNITS[1])
                        with pool.If(nb == 2):
                            pool.wait_ge(e_w, 2 * p + 2)
                            pool.wait_ge(e_y, 4 * p + 4 + 3)
                            pool.sem_inc(e_go, 1)
                            scatter(pool, 0)
                            pool.wait_ge(e_y, 4 * p + 4 + 4)
                            pool.sem_inc(e_go, 1)
                            scatter(pool, 1)
                        with pool.If(nb == 1):
                            pool.wait_ge(e_w, 2 * p + 2)
                            pool.wait_ge(e_y, 4 * p + 4 + 4)
                            pool.sem_inc(e_go, 1)
                            scatter(pool, 0)
                            pool.indirect_dma_start(spare_d, bass.IndirectOffsetOnAxis(ap=idx_s[:, 1:2], axis=0),
                                                    wcur[:, :], None).then_inc(e_scat, 16)
                        with pool.If(nb > 0):
                            nbn = pool.value_load(pass_tab[0:1, ds(2 * p + 3, 1)], min_val=0, max_val=2)
                            with pool.If(nbn == 0):
                                pool.wait_ge(e_scat, 32 * p + 64)
                                pool.sem_inc(e_go, 1)
            pool.memset(tiny[:, 0:1], 0.0).then_inc(e_end, 1)

            pool.wait_ge(e_end, 3)
            for t in range(TT):
                pool.wait_ge(f_a, t + 1)
                power(frs[:, t:t + 1], fss[:, t:t + 1], 1.0 / D, f_p, 2 * t, 1)

        @block.scalar
        def _(act):
            A = nc.scalar.activation
            tok_at = lambda t: slice(P * t, P * t + P)
            half = lambda h: slice(HS * h, HS * h + HS)

            def hi_unit(i):
                u = order.index(split[i])
                act.wait_ge(s_raw[u % 3], raw_count(u))
                if i >= 3:
                    done = (i - 3) // 2
                    if done < len(MIX):
                        act.wait_ge(s_z, first_group[done + 1])
                    else:
                        act.wait_ge(s_o, 3 * TT)
                A(whi[:, i % 3].rearrange("p k n -> p (k n)"), rawA[:, u % 3, :], ACT.Copy).then_inc(s_hi, 1)

            def copy_group(q, dst):
                act.wait_ge(s_z, q + 1)
                A(dst, bk[q % 3][:, :], ACT.Copy).then_inc(s_ze, 1)

            rows = 0

            def stream(point):
                nonlocal rows
                for what in POINTS[point]:
                    if what != "a":
                        hi_unit(what)
                        continue
                    i, rows = rows, rows + 1
                    act.wait_ge(s_adam, i + 1)
                    if i < NOW:
                        A(yT[:, i // 2, half(i % 2)], bk[i][:, :], ACT.Copy).then_inc(s_adac, 1)
                        continue
                    n = i - NOW
                    if n >= 2:
                        act.wait_ge(s_adad[n % 2], 16 * (n // 2))
                    A(modrow[0:1, n % 2, :], bk[3][0:1, :], ACT.Copy).then_inc(s_adac, 1)
                    act.wait_ge(s_adac, i + 1)
                    act.dma_start(mod_d[BANK * ADA[i]:BANK * ADA[i] + BANK].rearrange("(a n) -> a n", a=1),
                                  modrow[0:1, n % 2, :]).then_inc(s_adad[n % 2], 16)

            def square(t):
                act.wait_ge(s_x[t % 5], 16 * (t // 5 + 1))
                if t:
                    act.wait_ge(s_sq, t)
                A(T[:, 4, :], x_slot(t), ACT.Square, accum_out=ss[:, t:t + 1]).then_inc(s_sq, 1)

            square(0)
            square(1)
            stream("start")
            for t in range(2, 5):
                square(t)

            def z_token(t):
                if t == 2:
                    act.wait_ge(s_h0, 5)
                    act.wait_ge(s_sq, 5)
                if t == 4:
                    act.wait_ge(s_tp, 2 * TT)
                if t == 6:
                    act.wait_ge(s_sd, N_S)
                copy_group(t, Z_AT[t // 2][:, BANK * (t % 2):BANK * (t % 2) + BANK])

            for t in range(TT + 2):
                if 1 <= t <= TT:
                    for h in range(2):
                        q = 2 * (t - 1) + h
                        act.wait_ge(s_tp, q + 1)
                        A(hTh[:, 4 * h:4 * h + 4, tok_at(t - 1)],
                          bk[4 + q % 4][:, :].rearrange("p (k s) -> p k s", s=P), ACT.Copy).then_inc(s_thi, 1)
                if 5 <= t + 3 < TT:
                    square(t + 3)
                if 3 <= t < TT + 1:
                    z_token(t - 3)
            stream("h")
            act.wait_ge(s_par, 2)
            A(sp[:, 1, :], sp[:, 0, :], ACT.Exp, scale=-1.0).then_inc(s_sgc, 1)

            for b in range(TT // 2):
                if b == 1:
                    act.wait_ge(s_sq, TT)
                if b == 2:
                    act.wait_ge(s_tp, 2 * TT)
                if b == 3:
                    for t in (6, 7):
                        z_token(t)
                act.wait_ge(s_ze, 2 * b + 2)
                A(W_AT[b], Z_AT[b], ACT.Square).then_inc(s_sa, 1)
                if b == 0:
                    act.wait_ge(s_sgt, 1)
                    A(sgW[:, :, :].rearrange("p h t -> p (h t)"), bk[7][:, :], ACT.Copy).then_inc(s_sgc, 1)
                act.wait_ge(s_sd, N_S * b + 2)
                A(W_AT[b], W_AT[b], ACT.Tanh, scale=GELU_C).then_inc(s_sa, 1)
                if b == 0:
                    stream("gating")
            stream("mixing")
            Y = T[:, 0:2, :].rearrange("p a (t n) -> p (a t) n", n=WC)
            act.wait_ge(s_sd, 4 * N_S + 3 * TT + 2 + 4)
            for t in range(TT):
                if t:
                    act.wait_ge(s_sa, 8 + t)
                A(T[:, 2, 0:WC], Y[:, t, :], ACT.Square, accum_out=ssq[:, 2, t:t + 1]).then_inc(s_sa, 1)
            for j in range(2):
                for h in range(2):
                    act.wait_ge(s_st, 2 * j + h + 1)
                    A(yT[:, CJ + j, half(h)], bk[4 + 2 * j + h][:, :], ACT.Copy).then_inc(s_se, 1)

            def square_y(j):
                act.wait_ge(s_ld, N_LD * (j + 1))
                A(T[:, Y2[j], :], yT[:, 2 * CJ + j, :], ACT.Square).then_inc(s_sy, 1)

            def sums_out(n, k):
                act.wait_ge(s_ls, n + 1)
                A(ssq[:, k, :], bk[3][:, 0:TT], ACT.Copy).then_inc(s_ss, 1)

            for j in range(LJ):
                q0 = first_group[1 + j // 2] + 4 * (j % 2)
                if j == 0:
                    act.wait_ge(s_sa, 8 + TT)
                    act.wait_ge(s_st, 4)
                else:
                    act.wait_ge(s_ld, N_LD * j)
                for h in range(2):
                    copy_group(q0 + h, T[:, 0, half(h)])
                act.wait_ge(s_ze, q0 + 2)
                act.wait_ge(s_small, SMALL)
                if j:
                    act.wait_ge(s_lg, 2 * j)
                A(T[:, 1, :], T[:, 0, :], ACT.Identity, scale=cw[:, 3, j:j + 1], bias=cb[:, j:j + 1]).then_inc(s_la, 1)
                if j:
                    square_y(j - 1)
                for h in range(2):
                    copy_group(q0 + 2 + h, T[:, 4, half(h)])
                act.wait_ge(s_ld, N_LD * j + 3)
                act.wait_ge(s_par, PAR_DONE)
                act.wait_ge(s_lg, 2 * j + 1)
                for h in range(2):
                    A(T[:, 0, half(h)], bk[4 + h][:, :], ACT.Tanh, scale=0.5, bias=gateBh[:, 0, j:j + 1]).then_inc(s_la, 1)
                act.wait_ge(s_la, N_LA * j + 3)
                A(T[:, 3, :], T[:, 0, :], ACT.Tanh, scale=sp[:, 5, j:j + 1], bias=sp[:, 5, j:j + 1]).then_inc(s_la, 1)
                act.wait_ge(s_la, N_LA * j + 4)
                A(T[:, 0, :], T[:, 0, :], ACT.Exp, scale=sp[:, 0, j:j + 1], bias=sp[:, 0, j:j + 1]).then_inc(s_la, 1)
                A(T[:, 3, :], T[:, 3, :], ACT.Sqrt).then_inc(s_la, 1)
                act.wait_ge(s_lg, 2 * j + 2)
                if j:
                    act.wait_ge(s_ls, j)
                for h in range(2):
                    A(T[:, 2, half(h)], bk[6 + h][:, :], ACT.Tanh, scale=0.5, bias=gateBh[:, 1, j:j + 1]).then_inc(s_la, 1)
                if j:
                    sums_out(j - 1, 2 * CJ + j - 1)
                stream(f"lru{j}")
                act.wait_ge(s_ld, N_LD * j + 5)
                act.wait_ge(s_ze, q0 + 4)
                A(T[:, 3, :], T[:, 4, :], ACT.Square).then_inc(s_la, 1)
                act.wait_ge(s_ld, N_LD * j + 9)
                A(T[:, 3, :], T[:, 3, :], ACT.Tanh, scale=GELU_C).then_inc(s_la, 1)
            square_y(LJ - 1)

            def y_high(k):
                A(hTh[:, k, :], yT[:, k, :], ACT.Copy, scale=mixg[:, k:k + 1]).then_inc(s_yh, 1)

            for j in range(CJ):
                q0 = first_group[1 + LJ // 2 + j]
                if j == 0:
                    act.wait_ge(s_ld, N_LD * LJ)
                else:
                    act.wait_ge(s_cd, N_CD * j)
                for a in range(3):
                    for h in range(2):
                        copy_group(q0 + 2 * a + h, T[:, a, half(h)])
                act.wait_ge(s_cd, N_CD * j + 1)
                A(T[:, 3, :], T[:, 1, :], ACT.Copy, scale=caw[:, 2, j:j + 1]).then_inc(s_ca, 1)
                sums_out(LJ - 1 + j, 2 * CJ + LJ - 1 if j == 0 else j - 1)
                stream(f"conv{j}")
                if j == CJ - 1:
                    act.wait_ge(s_z, len(groups))
                    act.wait_ge(s_se, 4)
                    for k in range(CJ, KT):
                        y_high(k)
                act.wait_ge(s_cd, N_CD * j + 4)
                act.wait_ge(s_ls, LJ + j)
                A(T[:, 4, :], yT[:, j, :], ACT.Square).then_inc(s_ca, 1)
            sums_out(LJ + CJ - 1, CJ - 1)
            assert rows == len(ADA)

            for k in range(CJ):
                y_high(k)
            for i in range(2 * TT):
                n, t = divmod(i, TT)
                act.wait_ge(s_o, 3 * i + 1)
                act.wait_ge(s_rgp, 6)
                if i == 0:
                    act.wait_ge(s_yl, KT)
                    act.wait_ge(s_ls, LJ + CJ)
                if i >= 2:
                    act.wait_ge(s_od, 4 * (i - 2) + 4)
                A(T[:, i % 2, 0:BANK], bk[3 * (i % 2)][:, :], ACT.Copy, scale=rg[:, 1, t:t + 1]).then_inc(s_oa, 1)
                if i == TT - 1:
                    stream("out0")

            act.wait_ge(s_od, 8 * TT)
            for t in range(TT + 1):
                if t < TT:
                    act.wait_ge(s_x2[t % 2], 16 * (t // 2 + 1))
                    if t:
                        act.wait_ge(s_sq2, t)
                    A(T[:, 4, :], T[:, t % 2, :], ACT.Square, accum_out=ss[:, t:t + 1]).then_inc(s_sq2, 1)
                if t >= 1:
                    for h in range(2):
                        q = 2 * (t - 1) + h
                        act.wait_ge(s_tp2, q + 1)
                        if h == 0 and t >= 3:
                            act.wait_ge(s_lgm, t - 2)
                        A(h2T[(t - 1) % 2][:, 4 * h:4 * h + 4, :], bk[q % 4][:, :].rearrange("p (k s) -> p k s", s=P),
                          ACT.Copy).then_inc(s_tc2, 1)
            def hi(p, v):
                act.wait_ge(e_raw[v % 6], raw5(p, v))
                w = v - 4
                if w == 8 or w == 9:
                    act.wait_ge(e_unit, 6 * p + w - 3)
                elif w == 10:
                    act.wait_ge(e_main2, 4 * p + 2)
                elif w >= 0 and w % 2 == 0:
                    act.wait_ge(e_unit, 6 * p + w // 2 + 1)
                elif w >= 0:
                    act.wait_ge(e_main, 8 * p + w + 1)
                src = (rawA if v % 6 < 3 else rawB)[:, v % 3, :]
                A(unit_hi(v), src, ACT.Copy).then_inc(e_hi, 1)

            def x_hi(p, blk):
                for h in range(2):
                    j = 2 * blk + h
                    act.wait_ge(e_xtp, 4 * p + j + 1)
                    A(xTh[:, blk, 4 * h:4 * h + 4, :], bk[4 + h][:, :].rearrange("p (k s) -> p k s", s=P),
                      ACT.Copy).then_inc(e_xth, 1)

            act.wait_ge(s_r, 1)
            A(w4.rearrange("p t k -> p (t k)"), dv.rearrange("p t k -> p (t k)"), ACT.Exp).then_inc(s_re, 1)
            for t in range(TT):
                if t in (1, 3, 5):
                    if t == 1:
                        act.wait_ge(s_o, 6 * TT)
                    hi(0, t // 2)
                act.wait_ge(s_wdt, t + 1)
                if t:
                    act.wait_ge(s_b2m, 2 * t)
                A(WdT[0:E, :], bk[7][0:E, 0:P], ACT.Copy).then_inc(s_wdc, 1)
                for n in range(2):
                    i = 2 * t + n
                    act.wait_ge(s_b2m, i + 1)
                    if i >= 2:
                        act.wait_ge(s_b2d[i % 2], 16 * (i // 2))
                    A(stage[:, i % 2, :], bk[5 + n][:, :], ACT.Copy).then_inc(s_b2c, 1)
                    act.wait_ge(s_b2c, i + 1)
                    act.dma_start(acc_d[P * t:P * t + P, BANK * n:BANK * n + BANK], stage[:, i % 2, :])\
                       .then_inc(s_b2d[i % 2], 16)

            act.sem_inc(e_y, 4)
            x_hi(0, 0)
            x_hi(0, 1)

            def body(p, nb):
                nbn = act.value_load(pass_tab[0:1, ds(2 * p + 3, 1)], min_val=0, max_val=2)
                inc = 3 - nb
                at = lambda i, blk: 2 * i + (blk + 1) * inc
                blocks = range(nb)
                for v in range(12):
                    if v in (2, 6):
                        hi(p, v + 3)
                        i = (v - 2) // 4
                        for blk in blocks:
                            act.wait_ge(e_g, 4 * p + at(i, blk))
                            A(th[:, blk, :], g_sb[:, blk, :], ACT.Tanh, scale=ALPHA / 2).then_inc(e_th, inc)
                        continue
                    if v in (7, 9):
                        i = 0 if v == 7 else 1
                        for blk in blocks:
                            act.wait_ge(e_htp, 4 * p + at(i, blk))
                            A(HTh[:, blk, 4 * i:4 * i + 4, :], bk[6 + blk][:, :].rearrange("p (k s) -> p k s", s=P),
                              ACT.Copy).then_inc(e_hth, inc)
                    if v == 8:
                        x_hi(p + 1, 0)
                    if v == 11:
                        y_out(p, 0, nb)
                        with act.If(nbn == 2):
                            x_hi(p + 1, 1)
                        with act.If(nbn < 2):
                            act.wait_ge(e_xth, 4 * p + 6)
                            act.sem_inc(e_xth, 2)
                    hi(p, v + 3)
                y_out(p, 1, nb)

            def y_out(p, ch, nb):
                inc = 3 - nb
                for blk in range(nb):
                    act.wait_ge(e_main2, 4 * p + 2 * ch + (blk + 1) * inc)
                    act.wait_ge(e_w, 2 * p + 2)
                    act.wait_ge(e_free, p + 1)
                    A(y_sb[:, blk, BANK * ch:BANK * ch + BANK], bk[2 * ch + blk][:, :], ACT.Copy,
                      scale=wcur[:, blk:blk + 1]).then_inc(e_y, inc)

            with act.Fori(0, NPASS // GROUP) as g:
                live = act.value_load(pass_tab[0:1, ds(2 * GROUP * g + 1, 1)], min_val=0, max_val=2)
                with act.If(live > 0):
                    with act.Fori(0, GROUP) as i:
                        p = GROUP * g + i
                        nb = act.value_load(pass_tab[0:1, ds(2 * p + 1, 1)], min_val=0, max_val=2)
                        with act.If(nb == 2):
                            body(p, 2)
                        with act.If(nb == 1):
                            body(p, 1)
            A(tiny[:, 1:2], mhalf[:, 0:1], ACT.Copy).then_inc(e_end, 1)

            act.wait_ge(e_end, 3)
            for t in range(TT):
                act.wait_ge(f_d, 2 * t + 2)
                if t:
                    act.wait_ge(f_a, t)
                A(fsq[:, :], fx[:, t, :], ACT.Square, accum_out=fss[:, t:t + 1]).then_inc(f_a, 1)

        @block.vector
        def _(dve):
            V = nc.vector
            half = lambda h: slice(HS * h, HS * h + HS)
            tok_at = lambda t: slice(P * t, P * t + P)
            lows = 0
            sums = 0
            adap = 0

            def ada_sum(i):
                nonlocal adap
                dst = acc[:, i // 2, :]
                for h in range(2):
                    u = order.index(("ada", ADA[i], h))
                    dve.wait_ge(s_raw[u % 3], raw_count(u))
                    for k in range(KU):
                        w = rawA[:, u % 3, BANK * k:BANK * k + BANK]
                        ck = ccol[:, KU * h + k:KU * h + k + 1]
                        if h == 0 and k == 0:
                            ins = V.tensor_scalar(dst, w, ck, None, ALU.mult)
                        else:
                            if k:
                                dve.wait_ge(s_adap, adap)
                            else:
                                dve.wait_ge(s_used, freed[u - 1][1])
                            ins = V.scalar_tensor_tensor(dst, w, ck, dst, ALU.mult, ALU.add)
                        if k < KU - 1:
                            ins.then_inc(s_adap, 1)
                            adap += 1
                    ins.then_inc(s_used, 1)

            def stream(point):
                nonlocal lows, sums
                for what in POINTS[point]:
                    if what == "a":
                        if not on_pe(sums):
                            ada_sum(sums)
                        sums += 1
                        continue
                    assert what == lows
                    dve.wait_ge(s_hi, lows + 1)
                    V.tensor_tensor(wlo[:, lows % 3].rearrange("p k n -> p (k n)"), rawA[:, order.index(split[lows]) % 3, :],
                                    whi[:, lows % 3].rearrange("p k n -> p (k n)").bitcast(f32),
                                    ALU.subtract).then_inc(s_used, 1)
                    lows += 1

            V.memset(gateW[0:64, :, :, 64:P], 0.0)
            V.memset(gateW[64:P, :, :, 0:64], 0.0).then_inc(s_par, 1)
            dve.wait_ge(s_ccol, 16)
            stream("start")
            dve.wait_ge(s_bc, 16)
            dve.wait_ge(s_adac, NOW)
            V.scalar_tensor_tensor(yT[:, 1, :], yT[:, 1, :], 1.0, yT[:, 2, :], ALU.add, ALU.mult).then_inc(s_A, 1)
            dve.wait_ge(s_A, 1)

            def h_low(t):
                for h in range(2):
                    q = 2 * t + h
                    dve.wait_ge(s_thi, q + 1)
                    V.tensor_tensor(hTl[:, 4 * h:4 * h + 4, tok_at(t)], bk[4 + q % 4][:, :].rearrange("p (k s) -> p k s", s=P),
                                    hTh[:, 4 * h:4 * h + 4, tok_at(t)].bitcast(f32), ALU.subtract).then_inc(s_tlo, 1)

            for t in range(TT):
                dve.wait_ge(s_rp, 2 * t + 2)
                dve.wait_ge(s_x[t % 5], 16 * (t // 5 + 1))
                if t >= 2:
                    dve.wait_ge(s_tp, 2 * (t - 2) + 2)
                V.scalar_tensor_tensor(T[:, 2 + t % 2, :], x_slot(t), rs[:, t:t + 1], yT[:, 1, :],
                                       ALU.mult, ALU.mult).then_inc(s_h0, 1)
                dve.wait_ge(s_h0, t + 1)
                V.tensor_tensor(T[:, 2 + t % 2, :], T[:, 2 + t % 2, :], yT[:, 0, :], ALU.add).then_inc(s_h, 1)
                if t >= 1:
                    h_low(t - 1)
                if t == 3:
                    dve.wait_ge(s_small, SMALL)
                    V.scalar_tensor_tensor(sp[:, 0, :], lamc[:, :], -1.0, lamc[:, :], ALU.mult, ALU.max).then_inc(s_par, 1)
            h_low(TT - 1)
            stream("h")

            U_ = yT[:, 2 * CJ:2 * CJ + 2, :].rearrange("p a (t n) -> p (a t) n", n=WC)
            V_ = yT[:, 2 * CJ + 2:2 * CJ + 4, :].rearrange("p a (t n) -> p (a t) n", n=WC)
            sd = 0

            def slink(ins):
                nonlocal sd
                ins.then_inc(s_sd, 1)
                sd += 1
                dve.wait_ge(s_sd, sd)

            for b in range(TT // 2):
                z, w = Z_AT[b], W_AT[b]
                dve.wait_ge(s_sa, 2 * b + 1)
                slink(V.tensor_scalar(w, w, GELU_A, 1.0, ALU.mult, ALU.add))
                slink(V.tensor_tensor(w, w, z, ALU.mult))
                dve.wait_ge(s_sa, 2 * b + 2)
                slink(V.scalar_tensor_tensor(w, w, 1.0, z, ALU.add, ALU.mult))
                g = w.rearrange("p (t n) -> p t n", n=2 * WC)
                slink(V.tensor_scalar(U_[:, 2 * b:2 * b + 2, :], g[:, :, 0:WC], 0.5, None, ALU.mult))
                slink(V.tensor_scalar(V_[:, 2 * b:2 * b + 2, :], g[:, :, WC:2 * WC], 0.5, None, ALU.mult))
                if b == 0:
                    stream("gating")
            stream("mixing")
            for t in range(TT):
                V.bn_stats(bnst[:, t, :], V_[:, t, :]).then_inc(s_sd, 1)
            sd += TT
            for t in range(TT):
                dve.wait_ge(s_sd, sd)
                V.bn_aggr(mv[:, t, :], bnst[:, t, :]).then_inc(s_sd, 1)
            sd += TT
            dve.wait_ge(s_sp, 2)
            for t in range(TT):
                V.tensor_scalar(V_[:, t, :], V_[:, t, :], mv[:, t, 0:1], rs[:, t:t + 1], ALU.subtract,
                                ALU.mult).then_inc(s_sd, 1)
            sd += TT
            dve.wait_ge(s_sd, sd)
            dve.wait_ge(s_lng, 32)
            slink(V.tensor_tensor(V_, V_, lng[:, 0:1, :].to_broadcast([P, TT, WC]), ALU.mult))
            slink(V.tensor_tensor(V_, V_, lng[:, 1:2, :].to_broadcast([P, TT, WC]), ALU.add))
            assert sd == 4 * N_S + 3 * TT + 2
            Y = T[:, 0:2, :].rearrange("p a (t n) -> p (a t) n", n=WC)
            for h in range(4):
                dve.wait_ge(s_sm, h + 1)
                V.scalar_tensor_tensor(Y[:, :, 64 * h:64 * h + 64], bk[4 + h][:, :].rearrange("p (t n) -> p t n", n=64),
                                       sgB[:, h:h + 1], U_[:, :, 64 * h:64 * h + 64], ALU.add,
                                       ALU.mult).then_inc(s_sd, 1)
            sd += 4

            par = 2

            def plink(ins):
                nonlocal par
                ins.then_inc(s_par, 1)
                par += 1
                dve.wait_ge(s_par, par)

            dve.wait_ge(s_sgc, 1)
            plink(V.tensor_scalar(sp[:, 2, :], sp[:, 1, :], 2.0, None, ALU.add))
            plink(V.reciprocal(sp[:, 3, :], sp[:, 2, :]))
            plink(V.tensor_tensor(sp[:, 2, :], sp[:, 1, :], sp[:, 3, :], ALU.mult))
            plink(V.tensor_tensor(sp[:, 3, :], sp[:, 2, :], sp[:, 2, :], ALU.mult))
            plink(V.tensor_scalar(sp[:, 4, :], sp[:, 3, :], 1.0 / (2 * TERMS + 1), None, ALU.mult))
            for n in range(TERMS - 1, 0, -1):
                plink(V.scalar_tensor_tensor(sp[:, 4, :], sp[:, 4, :], 1.0 / (2 * n + 1), sp[:, 3, :], ALU.add, ALU.mult))
            plink(V.scalar_tensor_tensor(sp[:, 4, :], sp[:, 4, :], 1.0, sp[:, 2, :], ALU.add, ALU.mult))
            plink(V.tensor_scalar(sp[:, 5, :], lamc[:, :], -1.0, 0.0, ALU.mult, ALU.max))
            plink(V.scalar_tensor_tensor(sp[:, 5, :], sp[:, 4, :], 2.0, sp[:, 5, :], ALU.mult, ALU.add))
            plink(V.tensor_scalar(sp[:, 5, :], sp[:, 5, :], 2.0, None, ALU.mult))
            plink(V.tensor_scalar(sp[:, 0, :], sp[:, 5, :], -2.0, None, ALU.mult))
            plink(V.tensor_scalar(gateBh[:, :, :], gateB[:, :, :], 0.5, None, ALU.mult))
            assert par == PAR_DONE, par

            N = SEQ
            for j in range(LJ):
                ld = N_LD * j

                def link(ins):
                    nonlocal ld
                    ins.then_inc(s_ld, 1)
                    ld += 1
                    dve.wait_ge(s_ld, ld)

                la = N_LA * j
                dve.wait_ge(s_la, la + 1)
                for k in (1, 2, 3):
                    link(V.scalar_tensor_tensor(T[:, 1, k:N], T[:, 0, 0:N - k], cw[:, 3 - k, j:j + 1], T[:, 1, k:N],
                                                ALU.mult, ALU.add))
                dve.wait_ge(s_la, la + 8)
                link(V.scalar_tensor_tensor(T[:, 2, :], T[:, 2, :], 1.0, T[:, 1, :], ALU.add, ALU.mult))
                link(V.tensor_tensor(T[:, 2, :], T[:, 2, :], T[:, 3, :], ALU.mult))
                link(V.scalar_tensor_tensor(T[:, 2, :], T[:, 0, :], 1.0, T[:, 2, :], ALU.add, ALU.mult))
                dve.wait_ge(s_lg, 2 * j + 2)
                link(V.tensor_tensor_scan(T[:, 1, :], T[:, 0, :], T[:, 2, :], 0.0, ALU.mult, ALU.add))
                stream(f"lru{j}")
                dve.wait_ge(s_la, la + 9)
                link(V.tensor_scalar(T[:, 3, :], T[:, 3, :], GELU_A, 1.0, ALU.mult, ALU.add))
                link(V.tensor_tensor(T[:, 3, :], T[:, 3, :], T[:, 4, :], ALU.mult))
                dve.wait_ge(s_la, la + 10)
                link(V.scalar_tensor_tensor(T[:, 3, :], T[:, 3, :], 1.0, T[:, 4, :], ALU.add, ALU.mult))
                if j == 0:
                    dve.wait_ge(s_sm, 4)
                    dve.wait_ge(s_se, 4)
                link(V.scalar_tensor_tensor(yT[:, 2 * CJ + j, :], T[:, 3, :], 0.25, T[:, 1, :], ALU.mult, ALU.mult))
                assert ld == N_LD * (j + 1)

            for j in range(CJ):
                cd = N_CD * j
                q0 = first_group[1 + LJ // 2 + j]

                def clink(ins):
                    nonlocal cd
                    ins.then_inc(s_cd, 1)
                    cd += 1
                    dve.wait_ge(s_cd, cd)

                dve.wait_ge(s_ze, q0 + 6)
                clink(V.tensor_tensor(T[:, 1, :], T[:, 1, :], T[:, 2, :], ALU.mult))
                dve.wait_ge(s_ca, N_CA * j + 1)
                for k in (1, 2):
                    clink(V.scalar_tensor_tensor(T[:, 3, k:N], T[:, 1, 0:N - k], caw[:, 2 - k, j:j + 1], T[:, 3, k:N],
                                                 ALU.mult, ALU.add))
                stream(f"conv{j}")
                clink(V.tensor_tensor(yT[:, j, :], T[:, 3, :], T[:, 0, :], ALU.mult))

            def y_low(k, n):
                dve.wait_ge(s_yh, n)
                V.scalar_tensor_tensor(hTl[:, k, :], yT[:, k, :], mixg[:, k:k + 1], hTh[:, k, :].bitcast(f32),
                                       ALU.mult, ALU.subtract).then_inc(s_yl, 1)

            for k in range(CJ, KT):
                y_low(k, k - CJ + 1)
            for k in range(CJ):
                y_low(k, KT - CJ + k + 1)
            dve.wait_ge(s_ss, LJ + CJ)
            dve.wait_ge(s_sa, 8 + TT)
            V.tensor_tensor(rg[:, 0, :], ssq[:, 0, :], ssq[:, 1, :], ALU.add).then_inc(s_rg, 1)
            V.tensor_tensor(rg[:, 2, :], ssq[:, 4, :], ssq[:, 5, :], ALU.add).then_inc(s_rg, 1)
            for k in (6, 7):
                dve.wait_ge(s_rg, k - 4)
                V.tensor_tensor(rg[:, 2, :], rg[:, 2, :], ssq[:, k, :], ALU.add).then_inc(s_rg, 1)

            for i in range(2 * TT):
                n, t = divmod(i, TT)
                od = 4 * i

                def olink(ins):
                    nonlocal od
                    ins.then_inc(s_od, 1)
                    od += 1
                    dve.wait_ge(s_od, od)

                tt = T[:, i % 2, 0:BANK]
                dve.wait_ge(s_oa, i + 1)
                dve.wait_ge(s_o, 3 * i + 3)
                olink(V.scalar_tensor_tensor(tt, bk[3 * (i % 2) + 1][:, :], rg[:, 2, t:t + 1], tt, ALU.mult, ALU.add))
                olink(V.scalar_tensor_tensor(tt, bk[3 * (i % 2) + 2][:, :], rg[:, 0, t:t + 1], tt, ALU.mult, ALU.add))
                dve.wait_ge(s_gate1, 16)
                olink(V.tensor_tensor(tt, tt, T[:, 4, BANK * n:BANK * n + BANK], ALU.mult))
                dve.wait_ge(s_xo[i % 2], 16 * (i // 2 + 1))
                if i >= 2:
                    dve.wait_ge(s_x1[i % 2], 16 * (i // 2))
                olink(V.tensor_tensor(T[:, i % 2, BANK:2 * BANK], tt, T[:, 2 + i % 2, 0:BANK], ALU.add))
                if i == TT - 1:
                    stream("out0")
                    dve.wait_ge(s_bc2, 16 * 5)
                    V.scalar_tensor_tensor(yT[:, 1, :], yT[:, 1, :], 1.0, yT[:, 2, :], ALU.add, ALU.mult)\
                     .then_inc(s_A2, 1)
            assert lows == len(split)

            dve.wait_ge(s_A2, 1)

            def logits(t):
                dve.wait_ge(s_lgm, t + 1)
                V.tensor_tensor(lg[:, t, :], bk[4 + t % 2][:, 0:E], rb, ALU.add).then_inc(s_lgd, 1)

            for t in range(TT):
                dve.wait_ge(s_rp2, 2 * t + 2)
                dve.wait_ge(s_x2[t % 2], 16 * (t // 2 + 1))
                if t >= 2:
                    dve.wait_ge(s_tp2, 2 * (t - 2) + 2)
                    dve.wait_ge(s_h2d[t % 2], 16 * (t // 2))
                V.scalar_tensor_tensor(T[:, 2 + t % 2, :], T[:, t % 2, :], rs[:, t:t + 1], yT[:, 1, :],
                                       ALU.mult, ALU.mult).then_inc(s_g0, 1)
                dve.wait_ge(s_g0, t + 1)
                V.tensor_tensor(T[:, 2 + t % 2, :], T[:, 2 + t % 2, :], yT[:, 0, :], ALU.add).then_inc(s_g, 1)
                if t >= 2:
                    logits(t - 2)
            logits(TT - 2)
            logits(TT - 1)

            dve.wait_ge(s_lgd, TT)
            for t in range(TT):
                V.max(v8[:, t, :], lg[:, t, :]).then_inc(s_lgd, 1)
            dve.wait_ge(s_lgd, 2 * TT)
            for t in range(TT):
                V.max_index(i8[:, t, :], v8[:, t, :], lg[:, t, :]).then_inc(s_lgd, 1)
            r = 0

            def link(ins):
                nonlocal r
                ins.then_inc(s_r, 1)
                r += 1
                dve.wait_ge(s_r, r)

            n3 = lambda ap: ap.rearrange("p t k -> p (t k)")
            NC = TT * TOPK
            link(V.tensor_tensor(dv, v8[:, :, 0:TOPK], v8[:, :, 0:1].to_broadcast([P, TT, TOPK]), ALU.subtract))
            dve.wait_ge(s_lgd, 3 * TT)
            link(V.tensor_copy(i8f, i8[:, :, 0:TOPK]))
            dve.wait_ge(s_rc, 9)
            link(V.tensor_copy(iotaE, iotaEi))
            link(V.tensor_copy(pid, pidi))
            dve.wait_ge(s_tp2, 2 * TT)
            dve.wait_ge(s_h2d[0], 16 * (TT // 2))
            dve.wait_ge(s_h2d[1], 16 * (TT // 2))
            link(V.tensor_tensor(OH, iotaE.rearrange("p (a e) -> p a e", a=1).to_broadcast([P, NC, E]),
                                 n3(i8f).rearrange("p (n a) -> p n a", a=1).to_broadcast([P, NC, E]), ALU.is_equal))
            link(V.tensor_reduce(mask, OH.rearrange("p (t k) e -> p t e k", k=TOPK), AX.X, ALU.add))
            link(V.tensor_copy(maskb, mask))
            assert r == R_MASK
            dve.wait_ge(s_re, 1)
            link(V.tensor_reduce(sm, w4, AX.X, ALU.add))
            link(V.reciprocal(rsm, sm))
            link(V.tensor_tensor(w4, w4, rsm.rearrange("p (t a) -> p t a", a=1).to_broadcast([P, TT, TOPK]), ALU.mult))
            link(V.tensor_tensor(WOH, OH, n3(w4).rearrange("p (n a) -> p n a", a=1).to_broadcast([P, NC, E]), ALU.mult))
            link(V.tensor_reduce(Wd, WOH.rearrange("p (t k) e -> p t e k", k=TOPK), AX.X, ALU.add))
            assert r == R_WD
            link(V.tensor_scalar(pair[:, :, 1].bitcast(f32), n3(w4), 0.5, None, ALU.mult))
            link(V.tensor_copy(pair[:, :, 0].rearrange("p (t k) -> p t k", k=TOPK),
                               tok.rearrange("p (t a) -> p t a", a=1).to_broadcast([P, TT, TOPK])))
            dve.wait_ge(s_rk, 2)
            link(V.tensor_copy(cnt, bk[7][:, 256:256 + E]))
            link(V.tensor_scalar(npe, cnt, float(PASS), 1.0, ALU.is_gt, ALU.add))
            for k in range(2, SEQ // PASS):
                link(V.tensor_scalar(tmpe, cnt, float(PASS * k), None, ALU.is_gt))
                link(V.tensor_tensor(npe, npe, tmpe, ALU.add))
            link(V.tensor_tensor_scan(endp, onee, npe, 0.0, ALU.mult, ALU.add))
            link(V.tensor_tensor(begp, endp, npe, ALU.subtract))
            link(V.tensor_scalar(tmpe, begp, float(PASS), None, ALU.mult))
            link(V.tensor_tensor(slot, bk[7][:, 0:TT * E].rearrange("p (t e) -> p t e", e=E),
                                 tmpe.rearrange("p (a e) -> p a e", a=1).to_broadcast([P, TT, E]), ALU.add))
            for k in range(TOPK):
                o = OH.rearrange("p (t k) e -> p t k e", k=TOPK)[:, :, k, :]
                link(V.tensor_tensor(o, o, slot, ALU.mult))
            link(V.tensor_reduce(slf, OH, AX.X, ALU.add))
            link(V.tensor_copy(sli, slf))
            link(V.tensor_single_scalar(blki, sli, 7, ALU.logical_shift_right))
            link(V.tensor_single_scalar(remi, sli, P - 1, ALU.bitwise_and))
            link(V.scalar_tensor_tensor(loci, remi, float(NBLK), blki, ALU.mult, ALU.add))
            assert r == R_SLOT, r
            link(V.tensor_scalar(pm[:, 0, :], endp, pid, None, ALU.is_le))
            link(V.tensor_scalar(pm[:, 1, :], begp, pid, None, ALU.is_le))
            link(V.tensor_tensor(pm[:, 1, :], pm[:, 1, :], pm[:, 0, :], ALU.subtract))
            link(V.tensor_tensor(pm[:, 2, :], tmpe, cnt, ALU.add))
            link(V.tensor_scalar(pcol[:, 2:3], pid, float(PASS), float(P), ALU.mult, ALU.add))
            link(V.tensor_scalar(pm[:, 2, :], pm[:, 2, :], pcol[:, 2:3], None, ALU.is_gt))
            link(V.scalar_tensor_tensor(pm[:, 2, :], pm[:, 2, :], 1.0, pm[:, 1, :], ALU.add, ALU.mult))
            link(V.tensor_reduce(pcol[:, 0:1], pm[:, 0, :], AX.X, ALU.add))
            link(V.tensor_reduce(pcol[:, 1:2], pm[:, 2, :], AX.X, ALU.add))
            link(V.tensor_scalar(pcol[:, 0:1], pcol[:, 0:1], float(E - 1), None, ALU.min))
            link(V.tensor_copy(pcoli, pcol[:, 0:2]))
            assert r == R_PASS, r
            def lo(p, v):
                if v % 12 in POOL_UNITS:
                    return
                dve.wait_ge(e_hi, 12 * p + v + 1)
                V.tensor_tensor(unit_lo(v), (rawA if v % 6 < 3 else rawB)[:, v % 3, :], unit_hi(v).bitcast(f32),
                                ALU.subtract).then_inc(e_lo, 1)

            for v in range(3):
                lo(0, v)
            dve.wait_ge(s_tab, 16)
            st = T[:, 3, 0:2 * NBLK].rearrange("p (b c) -> p b c", c=2)
            V.tensor_copy(idx_tab[:, :], st[:, :, 0].bitcast(u32)).then_inc(s_tabc, 1)
            V.tensor_copy(wgt_tab[:, :], st[:, :, 1]).then_inc(s_tabc, 1)

            def x_lo(p, blk):
                for h in range(2):
                    dve.wait_ge(e_xth, 4 * p + 2 * blk + h + 1)
                    V.tensor_tensor(xTl[:, blk, 4 * h:4 * h + 4, :], bk[4 + h][:, :].rearrange("p (k s) -> p k s", s=P),
                                    xTh[:, blk, 4 * h:4 * h + 4, :].bitcast(f32), ALU.subtract).then_inc(e_xtl, 1)

            x_lo(0, 0)
            x_lo(0, 1)

            def body(p, nb):
                nbn = dve.value_load(pass_tab[0:1, ds(2 * p + 3, 1)], min_val=0, max_val=2)
                inc = 3 - nb
                at = lambda i, blk: 2 * i + (blk + 1) * inc
                blocks = range(nb)

                def bias(ch, blk):
                    dve.wait_ge(e_main, 8 * p + at(ch, blk))
                    dve.wait_ge(e_b1[ch % 2], 32 * p + 16 * (ch // 2 + 1))
                    i = ch // 2
                    if ch % 2 == 0:
                        dst = g_sb
                    else:
                        dst = u_sb
                    V.tensor_tensor(dst[:, blk, :], bk[2 * (ch % 2) + blk][:, :], b1s[:, ch % 2, :],
                                    ALU.add).then_inc(e_t, inc)

                for v in range(12):
                    i = v // 4
                    if v in (2, 6):
                        for blk in blocks:
                            if i:
                                dve.wait_ge(e_H, 4 * p + at(0, blk))
                            bias(2 * i, blk)
                            dve.wait_ge(e_t, 8 * p + at(2 * i, blk))
                            V.tensor_scalar(g_sb[:, blk, :], g_sb[:, blk, :], LIMIT, None, ALU.min).then_inc(e_g, inc)
                    if v in (3, 7):
                        for blk in blocks:
                            dve.wait_ge(e_th, 4 * p + at(i, blk))
                            V.scalar_tensor_tensor(g_sb[:, blk, :], th[:, blk, :], 1.0, g_sb[:, blk, :],
                                                   ALU.add, ALU.mult).then_inc(e_gs, inc)
                    if v in (4, 8):
                        i -= 1
                        for blk in blocks:
                            bias(2 * i + 1, blk)
                            dve.wait_ge(e_t, 8 * p + at(2 * i + 1, blk))
                            V.tensor_scalar(u_sb[:, blk, :], u_sb[:, blk, :], LIMIT, -LIMIT, ALU.min,
                                            ALU.max).then_inc(e_u, inc)
                            dve.wait_ge(e_u, 4 * p + at(i, blk))
                            dve.wait_ge(e_gs, 4 * p + at(i, blk))
                            V.scalar_tensor_tensor(u_sb[:, blk, :], u_sb[:, blk, :], 1.0, g_sb[:, blk, :],
                                                   ALU.add, ALU.mult).then_inc(e_H, inc)
                    if v in (7, 9):
                        i = 0 if v == 7 else 1
                        for blk in blocks:
                            dve.wait_ge(e_hth, 4 * p + at(i, blk))
                            V.tensor_tensor(HTl[:, blk, 4 * i:4 * i + 4, :],
                                            bk[6 + blk][:, :].rearrange("p (k s) -> p k s", s=P),
                                            HTh[:, blk, 4 * i:4 * i + 4, :].bitcast(f32), ALU.subtract)\
                                .then_inc(e_htl, inc)
                    if v == 10:
                        x_lo(p + 1, 0)
                    if v == 11:
                        with dve.If(nbn == 2):
                            x_lo(p + 1, 1)
                        with dve.If(nbn < 2):
                            dve.wait_ge(e_xtl, 4 * p + 6)
                            dve.sem_inc(e_xtl, 2)
                    lo(p, v + 3)

            with dve.Fori(0, NPASS // GROUP) as g:
                live = dve.value_load(pass_tab[0:1, ds(2 * GROUP * g + 1, 1)], min_val=0, max_val=2)
                with dve.If(live > 0):
                    with dve.Fori(0, GROUP) as i:
                        p = GROUP * g + i
                        nb = dve.value_load(pass_tab[0:1, ds(2 * p + 1, 1)], min_val=0, max_val=2)
                        with dve.If(nb == 2):
                            body(p, 2)
                        with dve.If(nb == 1):
                            body(p, 1)
            V.tensor_copy(tiny[:, 2:3], mhalf[:, 0:1]).then_inc(e_end, 1)

            dve.wait_ge(f_bc, 32)
            def total(t):
                dve.wait_ge(f_x[t], 32)
                V.tensor_tensor(fa[:, t, :], fa[:, t, :], fmod[:, 0, :], ALU.mult).then_inc(f_d, 1)
                dve.wait_ge(f_d, 2 * t + 1)
                V.tensor_tensor(fx[:, t, :], fx[:, t, :], fa[:, t, :], ALU.add).then_inc(f_d, 1)

            total(0)
            for t in range(TT):
                if t + 1 < TT:
                    total(t + 1)
                dve.wait_ge(f_p, 2 * t + 2)
                V.scalar_tensor_tensor(fa[:, t, :], fx[:, t, :], frs[:, t:t + 1], fmod[:, 1, :], ALU.mult,
                                       ALU.mult).then_inc(f_e, 1)

        @block.tensor
        def _(pe):
            mm = nc.tensor.matmul
            tok_at = lambda t: slice(P * t, P * t + P)
            half = lambda h: slice(HS * h, HS * h + HS)
            ada_unit = [u for u, o in enumerate(order) if o[0] == "ada" and o[2] == 1]
            split_unit = [u for u, o in enumerate(order) if o[0] != "ada"]
            sums = NOW

            def channel_sum(i):
                m = P if i < NOW else 1
                for h in range(2):
                    u = ada_unit[i] + h - 1
                    pe.wait_ge(s_raw[u % 3], raw_count(u))
                    for k in range(KU):
                        ck = ccol[:, KU * h + k:KU * h + k + 1]
                        last = mm(bk[min(i, 3)][0:m, :], ck.to_broadcast([P, m]), rawA[:, u % 3, BANK * k:BANK * k + BANK],
                                  start=h == 0 and k == 0, stop=False)
                    last.then_inc(s_usede, 1)

            def finish_sum(i):
                m = P if i < NOW else 1
                dst, n = bk[min(i, 3)][0:m, :], ADA[i]
                if not on_pe(i):
                    pe.wait_ge(*freed[ada_unit[i]])
                    mm(dst, ones[:, 0:m], acc[:, i // 2, :], start=True, stop=False)
                mm(dst, ident[0:NMOD * D // BANK, n:n + 1].to_broadcast([NMOD * D // BANK, m]), brows[:, :],
                   start=False, stop=True).then_inc(s_adam, 1)

            def stream(point):
                nonlocal sums
                for what in POINTS[point]:
                    if what == "a":
                        pe.wait_ge(s_adac, sums)
                        channel_sum(sums)
                        finish_sum(sums)
                        sums += 1

            def three(dst, pairs):
                last = None
                for i, ((ah, al), (bh, bl)) in enumerate(pairs):
                    mm(dst, ah, bh, start=i == 0, stop=False)
                    mm(dst, ah, bl, start=False, stop=False)
                    last = mm(dst, al, bh, start=False, stop=i == len(pairs) - 1)
                return last

            def group(q):
                i, a, b = groups[q]
                u = 2 * i
                wh = lambda k: whi[:, (u + k // KU) % 3, k % KU]
                wl = lambda k: wlo[:, (u + k // KU) % 3, k % KU]
                if q == first_group[i]:
                    pe.wait_ge(*freed[split_unit[u + 1]])
                if q >= 3:
                    pe.wait_ge(s_ze, q - 2)
                if a == "tok":
                    pairs = [((hTh[:, k, tok_at(b)], hTl[:, k, tok_at(b)]), (wh(k), wl(k))) for k in range(KT)]
                else:
                    c0 = slice(P * a, P * a + P)
                    pairs = [((wh(k)[:, c0], wl(k)[:, c0]), (hTh[:, k, half(b)], hTl[:, k, half(b)]))
                             for k in range(KT)]
                three(bk[q % 3][:, :], pairs).then_inc(s_z, 1)

            pe.wait_ge(s_const, 4)
            pe.wait_ge(s_ccol, 16)
            pe.wait_ge(s_brows, 16)
            channel_sum(1)
            for i in range(3):
                finish_sum(i)
            channel_sum(3)
            finish_sum(3)
            for t in range(TT + 1):
                if t < TT:
                    pe.wait_ge(s_h, t + 1)
                    for hf in range(2):
                        q = 2 * t + hf
                        if q >= 4:
                            pe.wait_ge(s_tlo, q - 3)
                        for k in range(4):
                            last = nc.tensor.transpose(bk[4 + q % 4][:, P * k:P * k + P],
                                                       T[:, 2 + t % 2, P * (4 * hf + k):P * (4 * hf + k) + P], ident[:, :])
                        last.then_inc(s_tp, 1)
                if t >= 1:
                    pe.wait_ge(s_tlo, 2 * t)
                    group(t - 1)
            pe.wait_ge(s_const, 5)
            for h in range(4):
                last = nc.tensor.transpose(bk[7][:, P * h:P * h + P], sgW[:, h, :], ident[:, :])
            last.then_inc(s_sgt, 1)
            stream("h")
            group(TT)
            stream("mixing")
            group(TT + 1)
            group(TT + 2)
            pe.wait_ge(s_sd, 4 * N_S + 3 * TT + 2)
            pe.wait_ge(s_sgc, 2)
            V_ = yT[:, 2 * CJ + 2:2 * CJ + 4, :].rearrange("p a (t n) -> p (a t) n", n=WC)
            for h in range(4):
                mm(bk[4 + h][:, :], sgW[:, h, :], V_[:, :, 64 * h:64 * h + 64], start=True, stop=True).then_inc(s_sm, 1)
            Y = T[:, 0:2, :].rearrange("p a (t n) -> p (a t) n", n=WC)
            pe.wait_ge(s_sd, 4 * N_S + 3 * TT + 2 + 4)
            for j in range(2):
                for hf in range(2):
                    for t in range(4):
                        last = nc.tensor.transpose(bk[4 + 2 * j + hf][:, P * t:P * t + P],
                                                   Y[:, 4 * hf + t, P * j:P * j + P], ident[:, :])
                    last.then_inc(s_st, 1)

            def gates(j):
                pe.wait_ge(s_ld, N_LD * j + 3)
                if j == 0:
                    pe.wait_ge(s_se, 4)
                    pe.wait_ge(s_par, PAR_DONE)
                else:
                    pe.wait_ge(s_la, N_LA * j)
                for g in range(2):
                    for hf in range(2):
                        last = mm(bk[4 + 2 * g + hf][:, :], gateW[:, g, j, :], T[:, 1, half(hf)], start=True, stop=True)
                    last.then_inc(s_lg, 1)

            def squares(n, tile):
                pe.wait_ge(s_adac, sums)
                if n:
                    pe.wait_ge(s_ss, n)
                for t in range(TT):
                    last = mm(bk[3][:, t:t + 1], T[:, tile, tok_at(t)], ones[:, 0:1], start=True, stop=True)
                last.then_inc(s_ls, 1)

            q = TT + 3
            for j in range(LJ):
                q0 = first_group[1] + 4 * j
                while q < q0 + 4:
                    group(q)
                    q += 1
                gates(j)
                if j:
                    pe.wait_ge(s_sy, j)
                    squares(j - 1, Y2[j - 1])
                    pe.wait_ge(s_ss, j)
                stream(f"lru{j}")
                while q < q0 + 7:
                    group(q)
                    q += 1
            for j in range(CJ):
                q0 = first_group[1 + LJ // 2 + j]
                while q < q0 + 6:
                    group(q)
                    q += 1
                if j == 0:
                    pe.wait_ge(s_sy, LJ)
                    squares(LJ - 1, Y2[LJ - 1])
                    pe.wait_ge(s_ss, LJ)
                stream(f"conv{j}")
                while q < min(q0 + 9, len(groups)):
                    group(q)
                    q += 1
                pe.wait_ge(s_ca, N_CA * j + 2)
                squares(LJ + j, 4)

            for n in range(2):
                u = 2 * (len(MIX) + n)
                pe.wait_ge(*freed[split_unit[u + 1]])
                for t in range(TT):
                    i = n * TT + t
                    if i == 0:
                        pe.wait_ge(s_yl, KT - CJ)
                        pe.wait_ge(s_ze, len(groups))
                        pe.wait_ge(s_adac, len(ADA))
                        pe.wait_ge(s_ss, LJ + CJ - 1)
                    if i >= 2:
                        pe.wait_ge(s_od, 4 * (i - 2) + 2)
                        pe.wait_ge(s_oa, i - 1)
                    for a, (k0, k1) in enumerate(((CJ, 2 * CJ), (2 * CJ, KT), (0, CJ))):
                        if i == 0 and k0 == 0:
                            pe.wait_ge(s_yl, KT)
                        if i == 1 and a == 0:
                            pe.wait_ge(s_ss, LJ + CJ)
                        three(bk[3 * (i % 2) + a][:, :],
                              [((hTh[:, k, tok_at(t)], hTl[:, k, tok_at(t)]),
                                (whi[:, (u + k // KU) % 3, k % KU], wlo[:, (u + k // KU) % 3, k % KU]))
                               for k in range(k0, k1)]).then_inc(s_o, 1)

            def logits(t):
                pe.wait_ge(s_tc2, 2 * t + 2)
                if t == 0:
                    pe.wait_ge(s_bc2, 16 * 5)
                if t >= 2:
                    pe.wait_ge(s_lgd, t - 1)
                for k in range(KT):
                    last = mm(bk[4 + t % 2][:, 0:E], h2T[t % 2][:, k, :], rw[:, k, :], start=k == 0, stop=k == KT - 1)
                last.then_inc(s_lgm, 1)

            pe.wait_ge(s_od, 8 * TT)
            for t in range(TT):
                pe.wait_ge(s_g, t + 1)
                for hf in range(2):
                    q = 2 * t + hf
                    if q >= 4:
                        pe.wait_ge(s_tc2, q - 3)
                    for k in range(4):
                        last = nc.tensor.transpose(bk[q % 4][:, P * k:P * k + P],
                                                   T[:, 2 + t % 2, P * (4 * hf + k):P * (4 * hf + k) + P], ident[:, :])
                    last.then_inc(s_tp2, 1)
                if t >= 1:
                    logits(t - 1)
            logits(TT - 1)
            pe.wait_ge(s_r, R_MASK)
            pe.wait_ge(s_rc, 9)
            for t in range(TT):
                o = bk[7][:, E * t:E * t + E]
                for s in range(t):
                    mm(o, onesb, maskb[:, s, :], start=s == 0, stop=False)
                last = mm(o, Ub, maskb[:, t, :], start=t == 0, stop=True)
            last.then_inc(s_rk, 1)
            for t in range(TT):
                last = mm(bk[7][:, TT * E:TT * E + E], onesb, maskb[:, t, :], start=t == 0, stop=t == TT - 1)
            last.then_inc(s_rk, 1)
            pe.wait_ge(s_r, R_RANK)
            pe.wait_ge(s_b2, 16)
            for t in range(TT):
                if t:
                    pe.wait_ge(s_wdc, t)
                nc.tensor.transpose(bk[7][0:E, 0:P], Wd[:, t, :], ident[:, :]).then_inc(s_wdt, 1)
                pe.wait_ge(s_wdc, t + 1)
                for n in range(2):
                    i = 2 * t + n
                    if i >= 2:
                        pe.wait_ge(s_b2c, i - 1)
                    mm(bk[5 + n][:, :], WdT[0:E, :], b2s[:, BANK * n:BANK * n + BANK], start=True, stop=True)\
                        .then_inc(s_b2m, 1)

            def x_transpose(p, blk):
                pe.wait_ge(e_gat, 32 * p + 32)
                for hf in range(2):
                    if blk:
                        pe.wait_ge(e_xtl, 4 * p + hf + 1)
                    for k in range(4):
                        last = nc.tensor.transpose(bk[4 + hf][:, P * k:P * k + P],
                                                   xg[:, blk, P * (4 * hf + k):P * (4 * hf + k) + P], ident[:, :])
                    last.then_inc(e_xtp, 1)

            pe.wait_ge(s_b2c, 2 * TT)
            x_transpose(0, 0)
            x_transpose(0, 1)

            def body(p, nb):
                nbn = pe.value_load(pass_tab[0:1, ds(2 * p + 3, 1)], min_val=0, max_val=2)
                inc = 3 - nb
                at = lambda i, blk: 2 * i + (blk + 1) * inc

                def products(v, blk, ah, al, ch, k0, end):
                    dst = bk[2 * (ch % 2) + blk][:, :]
                    for k in range(KU):
                        cols = slice(BANK * k, BANK * k + BANK)
                        wh, wl = unit_hi(v)[:, cols], unit_lo(v)[:, cols]
                        mm(dst, ah[:, blk, k0 + k, :], wh, start=k0 + k == 0, stop=False)
                        mm(dst, ah[:, blk, k0 + k, :], wl, start=False, stop=False)
                        last = mm(dst, al[:, blk, k0 + k, :], wh, start=False, stop=end and k == KU - 1)
                    return last

                def hidden_transpose(i):
                    for blk in range(nb):
                        pe.wait_ge(e_H, 4 * p + at(i, blk))
                        if i:
                            pe.wait_ge(e_htl, 4 * p + at(0, blk))
                        for k in range(4):
                            last = nc.tensor.transpose(bk[6 + blk][:, P * k:P * k + P],
                                                       u_sb[:, blk, P * k:P * k + P], ident[:, :])
                        last.then_inc(e_htp, inc)

                for v in range(12):
                    pe.wait_ge(*lo_count(p, v))
                    if v == 0:
                        pe.wait_ge(e_xtl, 4 * p + 4)
                    for blk in range(nb):
                        if v < 8:
                            ch, h = v // 2, v % 2
                            if h == 0 and ch < 2:
                                pe.wait_ge(e_y, 4 * p + 2 * ch + 2)
                            elif h == 0:
                                pe.wait_ge(e_t, 8 * p + at(ch - 2, blk))
                            end = products(v, blk, xTh, xTl, ch, KU * h, h == 1)
                            if h:
                                end.then_inc(e_main, inc)
                        else:
                            ch, h = (v - 8) % 2, (v - 8) // 2
                            if h == 0:
                                pe.wait_ge(e_t, 8 * p + at(2 + ch, blk))
                            pe.wait_ge(e_htl, 4 * p + at(h, blk))
                            end = products(v, blk, HTh, HTl, ch, KU * h, h == 1)
                            if h:
                                end.then_inc(e_main2, inc)
                        if h == 0 and blk == nb - 1:
                            end.then_inc(e_unit, 1)
                    if v == 5:
                        hidden_transpose(0)
                    if v == 7:
                        x_transpose(p + 1, 0)
                    if v == 8:
                        hidden_transpose(1)
                    if v == 10:
                        with pe.If(nbn == 2):
                            x_transpose(p + 1, 1)
                        with pe.If(nbn < 2):
                            pe.wait_ge(e_xtp, 4 * p + 6)
                            pe.sem_inc(e_xtp, 2)

            with pe.Fori(0, NPASS // GROUP) as g:
                live = pe.value_load(pass_tab[0:1, ds(2 * GROUP * g + 1, 1)], min_val=0, max_val=2)
                with pe.If(live > 0):
                    with pe.Fori(0, GROUP) as i:
                        p = GROUP * g + i
                        nb = pe.value_load(pass_tab[0:1, ds(2 * p + 1, 1)], min_val=0, max_val=2)
                        with pe.If(nb == 2):
                            body(p, 2)
                        with pe.If(nb == 1):
                            body(p, 1)


_INS = ("x", "c", "norm1_g", "norm2_g", "w_ada", "b_ada", "w_in", "conv_a_w", "sgu_w", "sgu_b", "sgu_ln_g",
        "sgu_ln_b", "conv_c_w", "conv_c_b", "rglru_gate_w", "rglru_gate_b", "rglru_lambda", "mix_norm_g",
        "w_out", "router_w", "router_b", "expert_w1", "expert_b1", "expert_w2", "expert_b2", "final_norm_g")
_OUTS = [((1, 1024, 1024), "float32")]


def kernel(**inputs):
    import numpy as _np
    import concourse.bacc as _bacc
    from concourse import mybir as _mybir
    from concourse.bass_utils import run_bass_kernel_spmd as _run

    nc = _bacc.Bacc("TRN2", target_bir_lowering=False, num_devices=1)
    arrays, args = {}, []
    for name in _INS:
        a = _np.ascontiguousarray(inputs[name])
        arrays[f"in_{name}_dram"] = a
        args.append(nc.dram_tensor(f"in_{name}_dram", a.shape, _mybir.dt.from_np(a.dtype), kind="ExternalInput").ap())
    for i, (shape, dtype) in enumerate(_OUTS):
        dt = _mybir.dt.from_np(_np.dtype(dtype))
        args.append(nc.dram_tensor(f"out_{i}_dram", shape, dt, kind="ExternalOutput").ap())
    decoder_kernel(nc, *args)
    r = _run(nc, [arrays], core_ids=[0])
    got = tuple(r.results[0][f"out_{i}_dram"] for i in range(len(_OUTS)))
    return got[0]
```
